# Optimizing a Trainium2 kernel written in Bass

```python
import jax, jax.numpy as jnp
from jax import lax
import numpy as np

D_MODEL = 2048
BATCH = 1
SEQ = 512
DEPTH = 1
DEC_BATCH = 8
DEC_SEQ = 1
PAST_LEN = 2048
PAGE_SIZE = 128

N_HEADS = 16
N_KV_HEADS = 2
HEAD_DIM = 64
GROUP = N_HEADS // N_KV_HEADS
ATTN_WIDTH = N_HEADS * HEAD_DIM
KV_WIDTH = N_KV_HEADS * HEAD_DIM
WINDOW = 128
BLOCK = WINDOW
ROPE_THETA = 10000.0
CONV_WIDTH = D_MODEL // 2
CONV_K = 3
D_FF = 5632
PLE_DIM = 256
RMS_EPS = 1e-6
IN_COLS = ATTN_WIDTH + 2 * KV_WIDTH + 3 * CONV_WIDTH + 2 * D_MODEL

kernel_name = "hybrid_swa_sink_shortconv_convffn_step"

def rmsnorm(x, g):
    xf = x.astype(jnp.float32)
    y = xf * lax.rsqrt(jnp.mean(xf * xf, axis=-1, keepdims=True) + RMS_EPS)
    return (y * g.astype(jnp.float32)).astype(x.dtype)

def rope(x, pos):
    half = HEAD_DIM // 2
    inv = ROPE_THETA ** (-jnp.arange(half, dtype=jnp.float32) / half)
    ang = pos.astype(jnp.float32)[:, None] * inv[None, :]
    cos = jnp.cos(ang)[None, :, None, :]
    sin = jnp.sin(ang)[None, :, None, :]
    xf = x.astype(jnp.float32)
    x1, x2 = xf[..., :half], xf[..., half:]
    return jnp.concatenate([x1 * cos - x2 * sin, x2 * cos + x1 * sin], axis=-1).astype(x.dtype)

def causal_dwconv(u, prev, w):
    full = jnp.concatenate([prev.astype(u.dtype), u], axis=1)
    T = u.shape[1]
    out = w[0] * full[:, 0:T]
    for k in range(1, CONV_K):
        out = out + w[k] * full[:, k:k + T]
    return out, full[:, -(CONV_K - 1):]

def sink_attention(q, k, v, mask, sinks):
    scale = HEAD_DIM ** -0.5
    s = jnp.einsum('nbqkgd,nbckd->nbkgqc', q, k).astype(jnp.float32) * scale
    s = jnp.where(mask[None, :, None, None], s, -jnp.inf)
    sink = sinks.astype(jnp.float32).reshape(N_KV_HEADS, GROUP)[None, None, :, :, None, None]
    sink = jnp.broadcast_to(sink, s.shape[:-1] + (1,))
    pr = jax.nn.softmax(jnp.concatenate([s, sink], axis=-1), axis=-1)[..., :-1]
    return jnp.einsum('nbkgqc,nbckd->nbqkgd', pr.astype(v.dtype), v)

def window_attention_prompt(q, k, v, sinks):
    N, T = q.shape[:2]
    nb = T // BLOCK
    qb = q.reshape(N, nb, BLOCK, N_KV_HEADS, GROUP, HEAD_DIM)
    kb = k.reshape(N, nb, BLOCK, N_KV_HEADS, HEAD_DIM)
    vb = v.reshape(N, nb, BLOCK, N_KV_HEADS, HEAD_DIM)

    def with_prev(xb):
        prev = jnp.pad(xb[:, :-1], ((0, 0), (1, 0), (0, 0), (0, 0), (0, 0)))
        return jnp.concatenate([prev, xb], axis=2)

    qi = jnp.arange(BLOCK)[:, None]
    ci = jnp.arange(2 * BLOCK)[None, :]
    rel = BLOCK + qi - ci
    band = (rel >= 0) & (rel < WINDOW)
    blk = jnp.arange(nb)[:, None, None]
    mask = band[None] & ((blk > 0) | (ci >= BLOCK)[None])
    o = sink_attention(qb, with_prev(kb), with_prev(vb), mask, sinks)
    return o.reshape(N, T, ATTN_WIDTH)

def window_attention_sample(q, k, v, buf_k, buf_v, sinks):
    N, T = q.shape[:2]
    kf = jnp.concatenate([buf_k.astype(k.dtype), k], axis=1)
    vf = jnp.concatenate([buf_v.astype(v.dtype), v], axis=1)
    qpos = PAST_LEN + jnp.arange(T)
    kpos = PAST_LEN - WINDOW + jnp.arange(WINDOW + T)
    rel = qpos[:, None] - kpos[None, :]
    mask = ((rel >= 0) & (rel < WINDOW))[None]
    o = sink_attention(q.reshape(N, 1, T, N_KV_HEADS, GROUP, HEAD_DIM), kf[:, None], vf[:, None], mask, sinks)
    return o.reshape(N, T, ATTN_WIDTH), kf[:, -WINDOW:], vf[:, -WINDOW:]

def layer(x, p, pos, prev_k, prev_v, prev_conv, prev_ffn, w, prompt):
    (g_mix_pre, g_mix_post, g_ffn_pre, g_ffn_post, w_in, sinks, conv_w, w_attn_branch,
     w_conv_branch, b_gate, w_o, w_ffn_up, ffn_conv_w, ffn_conv_b, w_ffn_down, w_ple, w_ple_gate) = w
    N, T = x.shape[:2]
    h = rmsnorm(x, g_mix_pre)
    proj = h @ w_in
    splits = [ATTN_WIDTH, ATTN_WIDTH + KV_WIDTH, ATTN_WIDTH + 2 * KV_WIDTH,
              ATTN_WIDTH + 2 * KV_WIDTH + CONV_WIDTH, ATTN_WIDTH + 2 * KV_WIDTH + 2 * CONV_WIDTH,
              ATTN_WIDTH + 2 * KV_WIDTH + 3 * CONV_WIDTH, ATTN_WIDTH + 2 * KV_WIDTH + 3 * CONV_WIDTH + D_MODEL]
    q, k, v, cb, cc, cu, ga, gb = jnp.split(proj, splits, axis=-1)
    q = rope(q.reshape(N, T, N_HEADS, HEAD_DIM), pos)
    k = rope(k.reshape(N, T, N_KV_HEADS, HEAD_DIM), pos)
    v = v.reshape(N, T, N_KV_HEADS, HEAD_DIM)
    if prompt:
        a = window_attention_prompt(q, k, v, sinks)
        new_k, new_v = k[:, -WINDOW:], v[:, -WINDOW:]
        prev_conv = jnp.zeros((N, CONV_K - 1, CONV_WIDTH), x.dtype)
        prev_ffn = jnp.zeros((N, CONV_K - 1, D_FF), x.dtype)
    else:
        a, new_k, new_v = window_attention_sample(q, k, v, prev_k, prev_v, sinks)
    conv_out, new_conv = causal_dwconv(cc * cu, prev_conv, conv_w)
    b_out = cb * conv_out
    branch_a = a @ w_attn_branch
    branch_b = b_out @ w_conv_branch
    merged = jax.nn.sigmoid(ga + b_gate[0]) * branch_a + jax.nn.sigmoid(gb + b_gate[1]) * branch_b
    x = x + rmsnorm(merged @ w_o, g_mix_post)
    h2 = rmsnorm(x, g_ffn_pre)
    up, gt = jnp.split(h2 @ w_ffn_up, 2, axis=-1)
    uc, new_ffn = causal_dwconv(up, prev_ffn, ffn_conv_w)
    f = (jax.nn.gelu(uc + ffn_conv_b, approximate=True) * gt) @ w_ffn_down
    x = x + rmsnorm(f, g_ffn_post)
    x = x + jax.nn.sigmoid(x @ w_ple_gate) * (p @ w_ple)
    return x, new_k, new_v, new_conv, new_ffn

def setup_inputs(seed: int = 0) -> dict:
    key = jax.random.key(seed)
    ks = jax.random.split(key, 26)
    f32 = jnp.float32

    def nrm(k, shape, scale=1.0):
        return jax.random.normal(k, shape, f32) * scale

    def gain(k):
        return 1.0 + 0.05 * jax.random.normal(k, (DEPTH, D_MODEL), f32)

    return {
        "x_prompt": nrm(ks[0], (BATCH, SEQ, D_MODEL)),
        "x_sample": nrm(ks[1], (DEC_BATCH, DEC_SEQ, D_MODEL)),
        "state_attn_k": nrm(ks[2], (DEPTH, DEC_BATCH, WINDOW, N_KV_HEADS, HEAD_DIM)),
        "state_attn_v": nrm(ks[3], (DEPTH, DEC_BATCH, WINDOW, N_KV_HEADS, HEAD_DIM)),
        "state_conv": nrm(ks[4], (DEPTH, DEC_BATCH, CONV_K - 1, CONV_WIDTH)),
        "state_ffn_conv": nrm(ks[5], (DEPTH, DEC_BATCH, CONV_K - 1, D_FF)),
        "p_prompt": nrm(ks[6], (DEPTH, BATCH, SEQ, PLE_DIM)),
        "p_sample": nrm(ks[7], (DEPTH, DEC_BATCH, DEC_SEQ, PLE_DIM)),
        "norm_mix_pre": gain(ks[8]),
        "norm_mix_post": gain(ks[9]),
        "norm_ffn_pre": gain(ks[10]),
        "norm_ffn_post": gain(ks[11]),
        "w_in": nrm(ks[12], (DEPTH, D_MODEL, IN_COLS), D_MODEL ** -0.5),
        "attn_sinks": nrm(ks[13], (DEPTH, N_HEADS), 0.5),
        "conv_w": nrm(ks[14], (DEPTH, CONV_K, CONV_WIDTH), CONV_K ** -0.5),
        "w_attn_branch": nrm(ks[15], (DEPTH, ATTN_WIDTH, D_MODEL), ATTN_WIDTH ** -0.5),
        "w_conv_branch": nrm(ks[16], (DEPTH, CONV_WIDTH, D_MODEL), CONV_WIDTH ** -0.5),
        "b_gate": nrm(ks[17], (DEPTH, 2, D_MODEL), 0.02),
        "w_o": nrm(ks[18], (DEPTH, D_MODEL, D_MODEL), D_MODEL ** -0.5),
        "w_ffn_up": nrm(ks[19], (DEPTH, D_MODEL, 2 * D_FF), D_MODEL ** -0.5),
        "ffn_conv_w": nrm(ks[20], (DEPTH, CONV_K, D_FF), CONV_K ** -0.5),
        "ffn_conv_b": nrm(ks[21], (DEPTH, D_FF), 0.02),
        "w_ffn_down": nrm(ks[22], (DEPTH, D_FF, D_MODEL), D_FF ** -0.5),
        "w_ple": nrm(ks[23], (DEPTH, PLE_DIM, D_MODEL), PLE_DIM ** -0.5),
        "w_ple_gate": nrm(ks[24], (DEPTH, D_MODEL, D_MODEL), D_MODEL ** -0.5),
    }

def reference(x_prompt, x_sample, state_attn_k, state_attn_v, state_conv, state_ffn_conv,
              p_prompt, p_sample, norm_mix_pre, norm_mix_post, norm_ffn_pre, norm_ffn_post,
              w_in, attn_sinks, conv_w, w_attn_branch, w_conv_branch, b_gate, w_o,
              w_ffn_up, ffn_conv_w, ffn_conv_b, w_ffn_down, w_ple, w_ple_gate):
    pos_prompt = jnp.arange(SEQ, dtype=jnp.int32)
    pos_sample = PAST_LEN + jnp.arange(DEC_SEQ, dtype=jnp.int32)
    xp, xs = x_prompt, x_sample
    kp_l, vp_l, cp_l, fp_l = [], [], [], []
    ks_l, vs_l, cs_l, fs_l = [], [], [], []
    for i in range(DEPTH):
        w = (norm_mix_pre[i], norm_mix_post[i], norm_ffn_pre[i], norm_ffn_post[i], w_in[i],
             attn_sinks[i], conv_w[i], w_attn_branch[i], w_conv_branch[i], b_gate[i], w_o[i],
             w_ffn_up[i], ffn_conv_w[i], ffn_conv_b[i], w_ffn_down[i], w_ple[i], w_ple_gate[i])
        xp, kp, vp, cp, fp = layer(xp, p_prompt[i], pos_prompt, None, None, None, None, w, True)
        xs, kss, vss, css, fss = layer(xs, p_sample[i], pos_sample, state_attn_k[i], state_attn_v[i],
                                       state_conv[i], state_ffn_conv[i], w, False)
        kp_l.append(kp); vp_l.append(vp); cp_l.append(cp); fp_l.append(fp)
        ks_l.append(kss); vs_l.append(vss); cs_l.append(css); fs_l.append(fss)
    new_k_p = jnp.stack(kp_l, 0)
    new_v_p = jnp.stack(vp_l, 0)
    new_c_p = jnp.stack(cp_l, 0)
    new_f_p = jnp.stack(fp_l, 0)
    new_k_s = jnp.stack(ks_l, 0)
    new_v_s = jnp.stack(vs_l, 0)
    new_c_s = jnp.stack(cs_l, 0)
    new_f_s = jnp.stack(fs_l, 0)
    return (xp, xs, new_k_p, new_v_p, new_c_p, new_f_p, new_k_s, new_v_s, new_c_s, new_f_s)


_drawn_inputs = setup_inputs


def setup_inputs(seed=0):
    import zlib

    import numpy as np

    out = dict(_drawn_inputs(seed))
    spreads = {}
    factors = {'attn_sinks': 8.0, 'b_gate': 8.0, 'ffn_conv_b': 5.062}
    for name, (base, spread) in spreads.items():
        noise = np.random.default_rng([zlib.crc32(name.encode()), seed]).standard_normal(out[name].shape)
        drawn = base * np.exp(spread * noise) if base else spread * noise
        out[name] = __import__('jax').numpy.asarray(drawn.astype(out[name].dtype))
    for name, factor in factors.items():
        out[name] = (out[name] * factor).astype(out[name].dtype)
    return out
```

```python
from contextlib import ExitStack

import concourse.bass as bass
from concourse import mybir
import numpy as np

P = 128
D = 2048
KD = D // P
TP, TS = 512, 8
T = TP + TS
HALF = T // 2
HD, NH, NKV, GRP = 64, 16, 2, 8
KA = NH * HD // P
FF = 5632
KF = FF // P
CH = 4
NCH = KF // CH
PLE = 256
KP = PLE // P
BLK = 128
NB = TP // BLK
EPS = 1e-6
SCALE = HD ** -0.5

Q_KV = 0
Q_Q = 2
Q_CONV = Q_Q + KA
Q_MERGE = Q_CONV + 3 * KA
Q_O = Q_MERGE + 3 * KD
Q_FFN = Q_O + KD
Q_CHUNK = 2 * CH + KD // 4
Q_PLE = Q_FFN + NCH * Q_CHUNK
Q_GATE = Q_PLE + 2
NQ = Q_GATE + KD
M_Q = 2
M_CONV = M_Q + KA
M_MERGE = M_CONV + 3 * KA
M_O = M_MERGE + 4 * KD
M_FFN = M_O + KD
M_CHUNK = 2 * CH + KD
M_GATE = M_FFN + NCH * M_CHUNK
C_MIXPRE, C_MIXPOST, C_FFNPRE, C_FFNPOST = 0, KD, 2 * KD, 3 * KD
C_CONVW = 4 * KD
C_BGATE = C_CONVW + 3 * KA
C_FCONVW = C_BGATE + 2 * KD
C_FCONVB = C_FCONVW + 3 * KF
NCHAN = C_FCONVB + KF


def build(nc, wstream, x_in, p_in, chan_in, sinkp_in, sinks_in, cstate_in, fstate_in, kcache_in,
          vcache_in, kstate_in, vstate_in, cst1_in, fst1_in, mats_in, rot_in, mask_in,
          y_out, kT_out, vT_out, ctail_out, ftail_out, kold_out, vold_out, cold_out, fold_out):
    f32, f32r = mybir.dt.float32, mybir.dt.float32r
    ALU, ACT, AX = mybir.AluOpType, mybir.ActivationFunctionType, mybir.AxisListType
    ds = bass.ds

    with ExitStack() as ctx:
        arena_base = -(-nc.sbuf_base // 64) * 64
        top = [arena_base]

        def region(nbytes):
            at = top[0]
            top[0] += -(-nbytes // 64) * 64
            return at

        def at(name, shape, offset, dt=f32):
            return nc.alloc_sbuf_tensor_at(name, [shape[0], *shape[1:]], dt, offset=offset)

        XB = T * 4
        r_wraw, r_whi, r_wlo = (region(4 * 4 * P * 4) for _ in range(3))
        r_hhi, r_hlo = region(KD * XB), region(KD * XB)
        r1, r2, r3 = region(KD * XB), region(KD * XB), region(KD * XB)

        w_raw = at("w_raw", [P, 4, 4 * P], r_wraw)
        w_hi = at("w_hi", [P, 4, 4 * P], r_whi, f32r)
        w_lo = at("w_lo", [P, 4, 4 * P], r_wlo, f32r)
        h_hi = at("h_hi", [P, KD, T], r_hhi, f32r)
        h_lo = at("h_lo", [P, KD, T], r_hlo, f32r)
        x_sb = at("x_sb", [P, KD, T], r1)
        a_hi = at("a_hi", [P, KA, T], r1, f32r)
        a_lo = at("a_lo", [P, KA, T], r1 + KA * XB, f32r)
        q_sb = at("q_sb", [P, KA, T], r1 + KA * XB)
        b_hi = at("b_hi", [P, KA, T], r2, f32r)
        b_lo = at("b_lo", [P, KA, T], r2 + KA * XB, f32r)
        y_sb = at("y_sb", [P, KD, T], r2)
        o = [r2]

        def sub(name, shape, dt=f32):
            t_ = at(name, shape, o[0], dt)
            o[0] += -(-int(np.prod(shape[1:])) // 8) * 32
            return t_

        cos = sub("cos", [P, T])
        sin = sub("sin", [P, T])
        rope_in = [sub(f"rope_in{i}", [P, T]) for i in range(2)]
        rope_s = sub("rope_s", [P, T])
        rope_c = sub("rope_c", [P, T])
        vT_sb = sub("vT_sb", [P, T])
        k_cache = sub("k_cache", [P, TS, BLK])
        v_cache = sub("v_cache", [P, TS, P])
        assert o[0] <= r2 + KD * XB
        o[0] = r3
        ss_sb = sub("ss_sb", [TS, NKV * TS, BLK])
        pTs_sb = sub("pTs_sb", [P, NKV * TS, TS])
        v_new = sub("v_new", [TS, P])
        cst_tmp = sub("cst_tmp", [P, KF, TS])
        cst_sb = sub("cst_sb", [P, KA, TS, 2])
        fst_sb = sub("fst_sb", [P, KF, TS, 2])
        assert o[0] <= r3 + KD * XB
        o[0] = r3
        s_sb = sub("s_sb", [P, 8, 2 * BLK])
        pT_sb = sub("pT_sb", [P, 4, 4 * BLK])
        q_blk = sub("q_blk", [P, KA, BLK])
        k_blk = sub("k_blk", [P, 2 * BLK])
        v_blk = sub("v_blk", [P, 2, P])
        mask_blk = sub("mask_blk", [P, 2 * BLK])
        c_sb = sub("c_sb", [P, T])
        zb = sub("zb", [P, T + 2])
        cv = sub("cv", [P, T])
        bt = sub("bt", [P, T])
        assert o[0] <= r3 + KD * XB, (o[0] - r3, KD * XB)
        merged = at("merged", [P, KD, T], r3)
        f_hi = at("f_hi", [P, CH, T], r3, f32r)
        f_lo = at("f_lo", [P, CH, T], r3 + CH * XB, f32r)
        o[0] = r3 + 2 * CH * XB
        fzb = sub("fzb", [P, T + 2])
        fcv = sub("fcv", [P, T])
        ge = sub("ge", [P, T])
        ge2 = sub("ge2", [P, T])
        ft = sub("ft", [P, T])
        p_raw = sub("p_raw", [P, KP, T])
        assert o[0] <= r3 + KD * XB
        ple_sb = at("ple_sb", [P, KD, T], r3)
        o[0] = top[0]
        chan = sub("chan", [P, NCHAN])
        ident = sub("ident", [P, P])
        rotm = sub("rotm", [P, P])
        ones = sub("ones", [P, P])
        rstd = sub("rstd", [P, T])
        sinkp = sub("sinkp", [P, NH])
        sinks = sub("sinks", [TS, NKV * TS])
        cs_s = sub("cs_s", [P, KA, TS])
        fs_s = sub("fs_s", [P, KF, TS])
        ctail = sub("ctail", [P, KA, TS + 2])
        ftail = sub("ftail", [P, KF, TS + 2])
        small = sub("small", [P, 6, 16])
        t0 = o[0]
        kT_sb = sub("kT_sb", [P, BLK + T])
        v_tok = sub("v_tok", [P, NB + 1, P])
        rstd2 = sub("rstd2", [P, T])
        sqacc1 = sub("sqacc1", [P, T])
        end = o[0]
        o[0] = t0
        ga_sb = sub("ga_sb", [P, T])
        gb_sb = sub("gb_sb", [P, T])
        ma_sb = sub("ma_sb", [P, T])
        mb_sb = sub("mb_sb", [P, T])
        end = max(end, o[0])
        o[0] = t0
        p_hi = sub("p_hi", [P, KP, T], f32r)
        p_lo = sub("p_lo", [P, KP, T], f32r)
        tt = [sub(f"tt{i}", [P, T]) for i in range(2)]
        end = max(end, o[0])
        sq_a = [at(f"sq_a{i}", [P, T], r3 + (14 + i) * XB) for i in range(2)]
        nv_a = at("nv_a", [P, T], r3 + 13 * XB)
        sq_b = [at(f"sq_b{i}", [P, T], t0 + i * XB) for i in range(2)]
        sqacc2 = at("sqacc2", [P, T], t0 + 2 * XB)
        nv_b = at("nv_b", [P, T], t0 + 3 * XB)
        sq_c = [at(f"sq_c{i}", [P, T], r3 + (10 + i) * XB) for i in range(2)]
        nv_c = at("nv_c", [P, T], r3 + 13 * XB)
        sqacc3 = at("sqacc3", [P, T], r3 + 14 * XB)
        assert end <= nc.sbuf_usable_end, (end, nc.sbuf_usable_end)

        pair = [ctx.enter_context(nc.psum_tensor(f"pair{i}", [P, 2, 512], f32)) for i in range(4)]
        bank = [pair[2][:, 0, :], pair[2][:, 1, :], pair[3][:, 0, :], pair[3][:, 1, :]]

        def both(i):
            return pair[i][:, :, 0:HALF]

        def two(ap):
            return ap.rearrange("p (h t) -> p h t", h=2)

        def sem(name):
            return ctx.enter_context(nc.semaphore(name))

        raw_ready = [sem(f"raw_ready{g}") for g in range(4)]
        hi_ready = sem("hi_ready")
        lo_ready = sem("lo_ready")
        w_used = sem("w_used")
        acc_free = sem("acc_free")
        in_ready = [sem(f"in_ready{i}") for i in range(4)]
        chan_ready = sem("chan_ready")
        tab_ready = sem("tab_ready")
        x_back = sem("x_back")
        p_ready = sem("p_ready")
        mask_ready = sem("mask_ready")
        rhs_hi = sem("rhs_hi")
        rhs_ready = sem("rhs_ready")
        sq_ready = sem("sq_ready")
        sq_added = sem("sq_added")
        acc_zero = sem("acc_zero")
        sum_ready = sem("sum_ready")
        inv_ready = sem("inv_ready")
        rstd_ready = sem("rstd_ready")
        dve_step = sem("dve_step")
        pool_set = sem("pool_set")
        rope_rot = sem("rope_rot")
        rope_sin = sem("rope_sin")
        rope_cos = sem("rope_cos")
        rope_done = sem("rope_done")
        v_turned = sem("v_turned")
        v_stored = sem("v_stored")
        v_placed = sem("v_placed")
        k_placed = sem("k_placed")
        ss_ready = sem("ss_ready")
        ss_shift = sem("ss_shift")
        ss_exp = sem("ss_exp")
        ss_prob = sem("ss_prob")
        ss_turned = sem("ss_turned")
        ss_copied = sem("ss_copied")
        ss_out = sem("ss_out")
        ss_hi = sem("ss_hi")
        staged = sem("staged")
        s_ready = sem("s_ready")
        m_ready = sem("m_ready")
        e_ready = sem("e_ready")
        prob_ready = sem("prob_ready")
        pT_ready = sem("pT_ready")
        pT_act = sem("pT_act")
        pT_dve = sem("pT_dve")
        pv_ready = sem("pv_ready")
        a_hi_ready = sem("a_hi_ready")
        a_ready = sem("a_ready")
        b_hi_ready = sem("b_hi_ready")
        b_ready = sem("b_ready")
        gate_out = sem("gate_out")
        merged_ready = sem("merged_ready")
        y_clear = sem("y_clear")
        y_used = sem("y_used")
        x_new = sem("x_new")
        p_split_hi = sem("p_split_hi")
        p_split = sem("p_split")
        fconv_ready = sem("fconv_ready")
        gelu_ready = sem("gelu_ready")
        f_hi_ready = sem("f_hi_ready")
        f_ready = sem("f_ready")
        ple_free = sem("ple_free")
        ple_done = sem("ple_done")
        sig_used = sem("sig_used")
        x_out = sem("x_out")
        out_done = sem("out_done")
        copy_done = sem("copy_done")
        tail_out = sem("tail_out")

        def rope_tile(r):
            return 1 if isinstance(r, int) and r == 0 else M_Q + r

        passed = sem("passed")

        def wait_alone(eng, semaphore, value):
            eng.wait_ge(semaphore, value)
            eng.sem_inc(passed, 1)

        block = ctx.enter_context(nc.Block())

        @block.sync
        def _(sp):
            for g in range(4):
                sp.dma_start(w_raw[:, g, :], wstream[0, g, :, :]).then_inc(raw_ready[g], 16)
            sp.dma_start(chan[:, :], chan_in).then_inc(chan_ready, 16)
            for i in range(4):
                sp.dma_start(x_sb[:, 4 * i:4 * i + 4, :], x_in[:, 4 * i:4 * i + 4, :])\
                  .then_inc(in_ready[i], 16)
            for dst, src in ((ident[:, :], mats_in[0, :, :]), (rotm[:, :], mats_in[1, :, :]),
                             (cos[:, :], rot_in[0, :, :]), (sin[:, :], rot_in[1, :, :]),
                             (sinkp[:, :], sinkp_in), (sinks[:, :], sinks_in),
                             (k_cache[:, :, 1:BLK], kcache_in), (v_cache[1:BLK, :, :], vcache_in),
                             (cst_sb[:, :, :, :], cstate_in), (fst_sb[:, :, :, :], fstate_in)):
                sp.dma_start(dst, src).then_inc(tab_ready, 16)
            for dst, src in ((kold_out, kstate_in), (vold_out, vstate_in),
                             (cold_out, cst1_in), (fold_out, fst1_in)):
                sp.dma_start(dst, src).then_inc(copy_done, 16)
            with sp.Fori(1, NQ) as q:
                for g in range(4):
                    sp.wait_ge(lo_ready, 4 * q + (g - 3))
                    sp.dma_start(w_raw[:, g, :],
                                 wstream[ds(q, 1), g, :, :].rearrange("a p n -> (a p) n"))\
                      .then_inc(raw_ready[g], 16)
            sp.wait_ge(copy_done, 64)

        @block.tensor
        def _(pe):
            def products(acc, slot, kk, rhi, rlo, k, start, stop):
                w = slice(kk * P, kk * P + P)
                for wt, r, first, last in ((w_hi, rhi, True, False), (w_hi, rlo, False, False),
                                           (w_lo, rhi, False, True)):
                    for h in range(2):
                        mm = pe.matmul(pair[acc][:, h, 0:HALF], wt[:, slot, w],
                                       r[:, k, h * HALF:(h + 1) * HALF],
                                       start=start and first, stop=stop and last)
                return mm

            def d_tile(q, m, acc, rows, wait_rows=True, rhi=h_hi, rlo=h_lo):
                if not (isinstance(m, int) and m < 2):
                    pe.wait_ge(acc_free, m - 1)
                for g in range(4):
                    pe.wait_ge(lo_ready, 4 * q + (g + 1))
                    for kk in range(4):
                        if wait_rows:
                            if rows == 0 and isinstance(q, int):
                                pe.wait_ge(rhs_ready, 4 * g + kk + 1)
                            elif kk == 0:
                                pe.wait_ge(rhs_ready, rows + 4 * g + 4)
                        mm = products(acc, g, kk, rhi, rlo, 4 * g + kk,
                                      g == 0 and kk == 0, g == 3 and kk == 3)
                    mm.then_inc(w_used, 1)

            def feature_sum(n, sqacc):
                pe.wait_ge(sq_added, 16 * n + 17)
                for h in range(2):
                    mm = pe.matmul(pair[2][:, h, 0:HALF], ones[:, :],
                                   sqacc[:, h * HALF:(h + 1) * HALF], start=True, stop=True)
                mm.then_inc(sum_ready, 1)

            def rotate(r, src):
                pe.wait_ge(acc_free, rope_tile(r))
                if not (isinstance(r, int) and r == 0):
                    pe.wait_ge(rope_sin, r)
                for h in range(2):
                    mm = pe.matmul(pair[3][:, h, 0:HALF], rotm[:, :],
                                   src[:, h * HALF:(h + 1) * HALF], start=True, stop=True)
                mm.then_inc(rope_rot, 1)

            d_tile(0, 0, 0, 0)
            pe.wait_ge(pool_set, 4)
            feature_sum(0, sqacc1)
            d_tile(1, 1, 1, 0, wait_rows=False)
            pe.wait_ge(tab_ready, 16 * 10)
            rotate(0, rope_in[0])
            pe.wait_ge(acc_free, 2)
            pe.wait_ge(inv_ready, 1)
            for b in range(NB):
                pe.transpose(bank[0][:, b * P:(b + 1) * P], vT_sb[:, b * P:(b + 1) * P], ident[:, :])
            pe.transpose(bank[1][0:TS, 0:P], vT_sb[:, TP:T], ident[:, :]).then_inc(v_turned, 1)

            def q_pair(i, first):
                for u in range(2):
                    t = 2 * i + u
                    d_tile(Q_Q + t, M_Q + t, u, 0, wait_rows=False)
                    if not (first and u == 0):
                        rotate(t, rope_in[u])
            q_pair(0, True)
            with pe.Fori(1, KA // 2) as i:
                q_pair(i, False)
            rotate(KA, rope_in[KA % 2])

            pe.wait_ge(rope_done, KA + 1)
            pe.wait_ge(k_placed, 1)
            pe.wait_ge(v_stored, 1)
            pe.wait_ge(rope_sin, KA + 1)
            for g in range(NKV):
                for n in range(TS):
                    mm = pe.matmul(bank[2 * g + n // 4][0:GRP, (n % 4) * P:(n % 4 + 1) * P],
                                   q_sb[HD * g:HD * g + HD, :, TP + n],
                                   k_cache[HD * g:HD * g + HD, n, :], start=True, stop=True)
            mm.then_inc(ss_ready, 1)
            pe.wait_ge(ss_prob, 1)
            for gn in range(NKV * TS):
                mm = pe.transpose(bank[0][:, gn * TS:(gn + 1) * TS], ss_sb[0:TS, gn, :],
                                  ident[0:TS, 0:TS])
            mm.then_inc(ss_turned, 1)
            pe.wait_ge(ss_copied, 1)
            pe.wait_ge(v_placed, 16)
            for g in range(NKV):
                for n in range(TS):
                    mm = pe.matmul(bank[1][HD * g:HD * g + HD, n * TS:(n + 1) * TS],
                                   v_cache[:, n, HD * g:HD * g + HD], pTs_sb[:, g * TS + n, :],
                                   start=True, stop=True)
            mm.then_inc(ss_out, 1)

            with pe.Fori(0, NB) as i:
                for u in range(2):
                    q = Q_CONV + 6 * i + 3 * u
                    m = M_CONV + 6 * i + 3 * u
                    pe.wait_ge(staged, 3 * i + 3)
                    if u == 0:
                        pe.wait_ge(a_ready, 2 * i + 1)
                    for j in (1, 2, 3, 0):
                        if j == 0:
                            pe.wait_ge(a_ready, 2 * i + (u + 1))
                        g, th = j // 2, j % 2
                        for v in range(2):
                            mm = pe.matmul(bank[j][:, v * 256:(v + 1) * 256],
                                           q_blk[HD * g:HD * g + HD, 4 * u + 2 * th + v, :],
                                           k_blk[HD * g:HD * g + HD, :], start=True, stop=True)
                        mm.then_inc(s_ready, 1)
                    d_tile(q, m, (3 * u) % 2, 0, wait_rows=False)
                    d_tile(q + 1, m + 1, (3 * u + 1) % 2, 0, wait_rows=False)
                    pe.wait_ge(prob_ready, 2 * i + (u + 1))
                    for g in range(NKV):
                        for j in range(2):
                            for t in range(4):
                                mm = pe.transpose(bank[2 * g + j][:, t * P:(t + 1) * P],
                                                  s_sb[:, 4 * g + t, j * P:(j + 1) * P],
                                                  ident[:, :])
                            mm.then_inc(pT_ready, 1)
                    d_tile(q + 2, m + 2, (3 * u + 2) % 2, 0, wait_rows=False)
                    pe.wait_ge(pT_act, 4 * i + (2 * u + 2))
                    pe.wait_ge(pT_dve, 4 * i + (2 * u + 2))
                    for g in range(NKV):
                        for j in range(2):
                            mm = pe.matmul(bank[0][HD * g:HD * g + HD, :],
                                           v_blk[:, j, HD * g:HD * g + HD],
                                           pT_sb[:, 2 * g + j, :], start=(j == 0), stop=(j == 1))
                    mm.then_inc(pv_ready, 1)

            with pe.Fori(0, KD) as i:
                q = Q_MERGE + 3 * i
                m = M_MERGE + 4 * i
                d_tile(q, m, 0, 0, wait_rows=False)
                d_tile(q + 1, m + 1, 1, 0, wait_rows=False)
                for half, (rhi, rlo, ready, n) in enumerate(
                        ((a_hi, a_lo, a_ready, 2 * NB + 1), (b_hi, b_lo, b_ready, KA))):
                    pe.wait_ge(acc_free, m + (1 + half))
                    pe.wait_ge(ready, n)
                    for g in range(2):
                        pe.wait_ge(lo_ready, 4 * q + (9 + 2 * half + g))
                        for kk in range(4):
                            mm = products(half, 2 * half + g, kk, rhi, rlo, 4 * g + kk,
                                          g == 0 and kk == 0, g == 1 and kk == 3)
                        mm.then_inc(w_used, 1)

            with pe.Fori(0, KD // 2) as i:
                for u in range(2):
                    d_tile(Q_O + 2 * i + u, M_O + 2 * i + u, u, KD)
            feature_sum(1, sqacc2)
            pe.wait_ge(inv_ready, 2)
            feature_sum(2, sqacc2)

            with pe.Fori(0, NCH) as c:
                with pe.Fori(0, CH) as t:
                    for u in range(2):
                        d_tile(Q_FFN + Q_CHUNK * c + 2 * t + u, M_FFN + M_CHUNK * c + 2 * t + u,
                               u, 2 * KD)
                with pe.Fori(0, KD // 4) as j:
                    for g in range(4):
                        pe.wait_ge(acc_free, M_FFN + M_CHUNK * c + 4 * j + (2 * CH + g - 1))
                        pe.wait_ge(lo_ready, 4 * (Q_FFN + Q_CHUNK * c + j) + (8 * CH + g + 1))
                        for kk in range(CH):
                            if g == 0:
                                pe.wait_ge(f_ready, CH * c + (kk + 1))
                            mm = products(g % 2, g, kk, f_hi, f_lo, kk, kk == 0, kk == CH - 1)
                        mm.then_inc(w_used, 1)

            pe.wait_ge(acc_free, M_GATE)
            pe.wait_ge(p_split, KP)
            for mt in range(KD):
                acc = (0, 1, 3)[mt % 3]
                if mt == 12:
                    feature_sum(3, sqacc3)
                if mt >= 3:
                    pe.wait_ge(ple_free, mt - 2)
                if mt % 2 == 0:
                    pe.wait_ge(lo_ready, 4 * Q_PLE + mt // 2 + 1)
                for kk in range(KP):
                    mm = products(acc, (mt // 2) % 4, 2 * (mt % 2) + kk, p_hi, p_lo, kk,
                                  kk == 0, kk == KP - 1)
                mm.then_inc(w_used if mt % 2 else ple_done, 1)
            pe.wait_ge(ple_free, KD)
            with pe.Fori(0, KD // 2) as i:
                for u in range(2):
                    d_tile(Q_GATE + 2 * i + u, M_GATE + 2 * i + u, u, 3 * KD)

        @block.scalar
        def _(act):
            def hi(q, slots=range(4)):
                for g in slots:
                    act.wait_ge(raw_ready[g], 16 * q + 16)
                    if not (isinstance(q, int) and q == 0):
                        act.wait_ge(w_used, 4 * q + (g - 3))
                    nc.scalar.activation(w_hi[:, g, :], w_raw[:, g, :], ACT.Copy)\
                      .then_inc(hi_ready, 1)

            def root(n):
                act.wait_ge(inv_ready, n + 1)
                src = (nv_a, nv_b, nv_b, nv_c)[n]
                nc.scalar.activation(rstd[:, :], src[:, :], ACT.Sqrt).then_inc(rstd_ready, 1)

            hi(0)
            act.wait_ge(chan_ready, 16)
            for part in range(4):
                act.wait_ge(in_ready[part], 16)
                with act.Fori(0, 2) as i:
                    for u in range(2):
                        k = 4 * part + 2 * i + u
                        nc.scalar.activation(h_hi[:, ds(k, 1), :].rearrange("p a t -> p (a t)"),
                                             x_sb[:, ds(k, 1), :].rearrange("p a t -> p (a t)"), ACT.Copy,
                                             scale=chan[:, ds(C_MIXPRE + k, 1)]).then_inc(rhs_hi, 1)
                        if part > 0:
                            wait_alone(act, sq_added, k)
                        else:
                            wait_alone(act, sq_added, 2 * i + 1)
                        nc.scalar.activation(sq_a[u][:, :], x_sb[:, ds(k, 1), :].rearrange("p a t -> p (a t)"),
                                             ACT.Square).then_inc(sq_ready, 1)
            hi(1)
            root(0)
            hi(2)
            with act.Fori(0, KA) as t:
                hi(Q_Q + 1 + t)
            act.wait_ge(ss_shift, 2)
            nc.scalar.activation(ss_sb[0:TS, :, :], ss_sb[0:TS, :, :], ACT.Exp).then_inc(ss_exp, 1)
            nc.scalar.activation(small[0:TS, 2, :], small[0:TS, 1, :], ACT.Exp).then_inc(ss_exp, 1)
            act.wait_ge(ss_out, 1)
            nc.scalar.activation(a_hi[:, :, TP:T],
                                 bank[1][:, 0:TS * GRP].rearrange("p (n t) -> p t n", n=TS),
                                 ACT.Copy).then_inc(ss_hi, 1)

            with act.Fori(0, NB) as i:
                for u in range(2):
                    q = Q_CONV + 6 * i + 3 * u
                    hi(q + 1)
                    act.wait_ge(m_ready, 2 * i + (u + 1))
                    for h in range(8):
                        nc.scalar.activation(s_sb[:, h, :], s_sb[:, h, :], ACT.Exp,
                                             bias=small[:, 1, h:h + 1],
                                             accum_out=small[:, 3, h:h + 1])
                    nc.scalar.activation(small[:, 4, 0:8], small[:, 2, 0:8], ACT.Exp)\
                      .then_inc(e_ready, 1)
                    hi(q + 2)
                    for j in range(2):
                        act.wait_ge(pT_ready, 8 * i + (4 * u + j + 1))
                        nc.scalar.activation(pT_sb[:, j, :], bank[j], ACT.Copy).then_inc(pT_act, 1)
                    hi(q + 3)
                    wait_alone(act, acc_free, M_CONV + 6 * i + (3 * u + 3))
                    nc.scalar.activation(b_hi[:, ds(2 * i + u, 1), :].rearrange("p a t -> p (a t)"),
                                         bt[:, :], ACT.Copy).then_inc(b_hi_ready, 1)
                    wait_alone(act, pv_ready, 2 * i + (u + 1))
                    nc.scalar.activation(a_hi[:, 4 * u:4 * u + 4, ds(i * BLK, BLK)],
                                         bank[0].rearrange("p (t s) -> p t s", t=4),
                                         ACT.Copy).then_inc(a_hi_ready, 1)

            with act.Fori(0, KD) as i:
                q = Q_MERGE + 3 * i
                hi(q + 1)
                for j, gate in enumerate((ga_sb, gb_sb)):
                    wait_alone(act, acc_free, M_MERGE + 4 * i + (j + 1))
                    nc.scalar.activation(gate[:, :], gate[:, :], ACT.Sigmoid,
                                         bias=chan[:, ds(C_BGATE + KD * j + i, 1)])\
                      .then_inc(gate_out, 1)
                    hi(q + (2 + j))
            with act.Fori(0, KD) as k:
                wait_alone(act, merged_ready, k + 1)
                nc.scalar.activation(h_hi[:, ds(k, 1), :].rearrange("p a t -> p (a t)"),
                                     merged[:, ds(k, 1), :].rearrange("p a t -> p (a t)"), ACT.Copy)\
                  .then_inc(rhs_hi, 1)

            with act.Fori(0, KD // 2) as i:
                for u in range(2):
                    m = 2 * i + u
                    hi(Q_O + 1 + m)
                    act.wait_ge(acc_free, M_O + m + 1)
                    wait_alone(act, sq_added, m + KD)
                    nc.scalar.activation(sq_b[u][:, :], y_sb[:, ds(m, 1), :].rearrange("p a t -> p (a t)"),
                                         ACT.Square).then_inc(sq_ready, 1)
            root(1)
            with act.Fori(0, KD // 2) as i:
                for u in range(2):
                    k = 2 * i + u
                    wait_alone(act, x_new, k + 1)
                    nc.scalar.activation(h_hi[:, ds(k, 1), :].rearrange("p a t -> p (a t)"),
                                         x_sb[:, ds(k, 1), :].rearrange("p a t -> p (a t)"), ACT.Copy,
                                         scale=chan[:, ds(C_FFNPRE + k, 1)]).then_inc(rhs_hi, 1)
                    wait_alone(act, sq_added, k + 2 * KD)
                    nc.scalar.activation(sq_b[u][:, :], x_sb[:, ds(k, 1), :].rearrange("p a t -> p (a t)"),
                                         ACT.Square).then_inc(sq_ready, 1)
            root(2)
            act.wait_ge(p_ready, 16)
            for k in range(KP):
                nc.scalar.activation(p_hi[:, k, :], p_raw[:, k, :], ACT.Copy).then_inc(p_split_hi, 1)

            with act.Fori(0, NCH) as c:
                with act.Fori(0, CH) as t:
                    q = Q_FFN + Q_CHUNK * c + 2 * t
                    hi(q + 1)
                    wait_alone(act, fconv_ready, CH * c + t + 1)
                    nc.scalar.activation(ge[:, :], fcv[:, :], ACT.Gelu_apprx_tanh,
                                         bias=chan[:, ds(C_FCONVB + CH * c + t, 1)])\
                      .then_inc(gelu_ready, 1)
                    hi(q + 2)
                    wait_alone(act, acc_free, M_FFN + M_CHUNK * c + 2 * t + 2)
                    nc.scalar.activation(f_hi[:, ds(t, 1), :].rearrange("p a t -> p (a t)"),
                                         ft[:, :], ACT.Copy).then_inc(f_hi_ready, 1)
                with act.Fori(0, KD // 4) as j:
                    hi(Q_FFN + Q_CHUNK * c + j + (2 * CH + 1))
            with act.Fori(0, KD // 2) as i:
                for u in range(2):
                    k = 2 * i + u
                    act.wait_ge(acc_free, M_GATE)
                    wait_alone(act, sq_added, k + 3 * KD)
                    nc.scalar.activation(sq_c[u][:, :], y_sb[:, ds(k, 1), :].rearrange("p a t -> p (a t)"),
                                         ACT.Square).then_inc(sq_ready, 1)
            hi(Q_PLE + 1)
            root(3)
            hi(Q_GATE)
            with act.Fori(0, KD) as k:
                wait_alone(act, x_new, k + (KD + 1))
                nc.scalar.activation(h_hi[:, ds(k, 1), :].rearrange("p a t -> p (a t)"),
                                     x_sb[:, ds(k, 1), :].rearrange("p a t -> p (a t)"), ACT.Copy)\
                  .then_inc(rhs_hi, 1)

            def gate(i, u, first=False, last=False):
                m = 2 * i + u
                if not last:
                    hi(Q_GATE + 1 + m)
                act.wait_ge(w_used, 4 * (Q_GATE + m) + 4)
                if not first:
                    act.wait_ge(sig_used, m)
                nc.scalar.activation(two(tt[0][:, :]), both(u), ACT.Sigmoid)\
                  .then_inc(acc_free, 1)
            gate(0, 0, first=True)
            gate(0, 1)
            with act.Fori(1, KD // 2 - 1) as i:
                gate(i, 0)
                gate(i, 1)
            gate(KD // 2 - 1, 0)
            gate(KD // 2 - 1, 1, last=True)

        @block.vector
        def _(dve):
            class Steps:
                base, k = 0, 0

                def at(self, base):
                    self.base, self.k = base, 0

                def done(self, ins):
                    ins.then_inc(dve_step, 1)
                    self.k += 1

                def wait(self):
                    dve.wait_ge(dve_step, self.base + self.k)
            st = Steps()

            def lo(q, slots=range(4)):
                for g in slots:
                    dve.wait_ge(hi_ready, 4 * q + (g + 1))
                    dve.tensor_tensor(w_lo[:, g, :], w_raw[:, g, :], w_hi[:, g, :].bitcast(f32),
                                      ALU.subtract).then_inc(lo_ready, 1)

            def complete(q):
                dve.wait_ge(w_used, 4 * q + 4)

            def scaled(dst, acc, by=rstd):
                return dve.tensor_tensor(two(dst), both(acc), two(by[:, :]), ALU.mult)

            def invert(n):
                dst = (nv_a, nv_b, nv_b, nv_c)[n]
                dve.wait_ge(sum_ready, n + 1)
                if n == 2:
                    dve.wait_ge(rstd_ready, 2)
                st.done(dve.tensor_scalar(two(dst[:, :]), both(2), 1.0 / D, EPS, ALU.mult, ALU.add))
                st.wait()
                dve.reciprocal(dst[:, :], dst[:, :]).then_inc(inv_ready, 1)

            def row(t_, k):
                return t_[:, ds(k, 1), :].rearrange("p a t -> p (a t)")

            def h_low(k, gain, count):
                dve.wait_ge(rhs_hi, count)
                dve.scalar_tensor_tensor(out=row(h_lo, k), in0=row(x_sb, k),
                                         scalar=chan[:, ds(gain + k, 1)],
                                         in1=row(h_hi, k).bitcast(f32),
                                         op0=ALU.mult, op1=ALU.subtract).then_inc(rhs_ready, 1)

            lo(0)
            dve.wait_ge(chan_ready, 16)
            for part in range(4):
                dve.wait_ge(in_ready[part], 16)
                with dve.Fori(0, 4) as i:
                    h_low(4 * part + i, C_MIXPRE, 4 * part + i + 1)
            dve.wait_ge(tab_ready, 16 * 10)
            for nb, wcol, state, dst in ((KA, C_CONVW, cst_sb, cs_s), (KF, C_FCONVW, fst_sb, fs_s)):
                st.wait()
                for j, o_ in ((0, dst), (1, cst_tmp)):
                    st.done(dve.tensor_tensor(
                        o_[:, 0:nb, :], state[:, :, :, j],
                        chan[:, wcol + nb * j:wcol + nb * (j + 1)].unsqueeze(2)
                        .to_broadcast([P, nb, TS]), ALU.mult))
                st.wait()
                st.done(dve.tensor_tensor(dst[:, 0:nb, :], dst[:, 0:nb, :], cst_tmp[:, 0:nb, :],
                                          ALU.add))
            lo(1)
            invert(0)
            complete(0)
            dve.wait_ge(rstd_ready, 1)
            scaled(rope_in[0][:, :], 0).then_inc(acc_free, 1)
            st.done(dve.tensor_tensor(rstd2[:, :], rstd[:, :], rstd[:, :], ALU.mult))

            def sine(r):
                dve.wait_ge(rope_rot, r + 1)
                if not (isinstance(r, int) and r == 0):
                    dve.wait_ge(rope_done, r)
                dve.tensor_tensor(two(rope_s[:, :]), both(3), two(sin[:, :]), ALU.mult)\
                   .then_inc(rope_sin, 1)
            lo(2)
            complete(1)
            scaled(vT_sb[:, :], 1).then_inc(acc_free, 1)
            sine(0)
            dve.wait_ge(v_turned, 1)
            st.done(dve.tensor_copy(v_tok[:, 1:NB + 1, :], bank[0].rearrange("p (b s) -> p b s", b=NB)))
            dve.tensor_copy(v_new[:, :], bank[1][0:TS, 0:P]).then_inc(v_stored, 1)

            def q_pair(i, first):
                for u in range(2):
                    t = 2 * i + u
                    lo(Q_Q + 1 + t)
                    complete(Q_Q + t)
                    dve.wait_ge(rope_done, t if not first else max(t, 1))
                    scaled(rope_in[(u + 1) % 2][:, :], u).then_inc(acc_free, 1)
                    if not (first and u == 0):
                        sine(t)
            q_pair(0, True)
            with dve.Fori(1, KA // 2) as i:
                q_pair(i, False)
            sine(KA)

            dve.wait_ge(rope_done, 1)
            dve.tensor_copy(k_cache[:, :, 0], kT_sb[:, BLK + TP:BLK + T]).then_inc(k_placed, 1)
            dve.wait_ge(ss_ready, 1)
            for j in range(4):
                st.done(dve.tensor_scalar(ss_sb[:, 4 * j:4 * j + 4, :],
                                          bank[j][0:TS, :].rearrange("p (n s) -> p n s", n=4),
                                          SCALE, None, ALU.mult))
            st.wait()
            NS = NKV * TS
            st.done(dve.tensor_reduce(small[0:TS, 0, :], ss_sb[:, :, :], AX.X, ALU.max))
            st.wait()
            st.done(dve.tensor_tensor(small[0:TS, 0, :], small[0:TS, 0, :], sinks[:, :], ALU.max))
            st.wait()
            dve.tensor_tensor(small[0:TS, 1, :], sinks[:, :], small[0:TS, 0, :], ALU.subtract)\
               .then_inc(ss_shift, 1)
            dve.tensor_tensor(ss_sb[:, :, :], ss_sb[:, :, :],
                              small[0:TS, 0, :].unsqueeze(2).to_broadcast([TS, NS, BLK]),
                              ALU.subtract).then_inc(ss_shift, 1)
            dve.wait_ge(ss_exp, 2)
            st.done(dve.tensor_reduce(small[0:TS, 3, :], ss_sb[:, :, :], AX.X, ALU.add))
            st.wait()
            st.done(dve.tensor_tensor(small[0:TS, 3, :], small[0:TS, 3, :], small[0:TS, 2, :], ALU.add))
            st.wait()
            st.done(dve.reciprocal(small[0:TS, 4, :], small[0:TS, 3, :]))
            st.wait()
            dve.tensor_tensor(ss_sb[:, :, :], ss_sb[:, :, :],
                              small[0:TS, 4, :].unsqueeze(2).to_broadcast([TS, NS, BLK]),
                              ALU.mult).then_inc(ss_prob, 1)
            dve.wait_ge(ss_turned, 1)
            dve.tensor_copy(pTs_sb[:, :, :], bank[0][:, 0:NS * TS].rearrange("p (a b) -> p a b", a=NS))\
               .then_inc(ss_copied, 1)
            dve.wait_ge(ss_hi, 1)
            dve.tensor_tensor(a_lo[:, :, TP:T],
                              bank[1][:, 0:TS * GRP].rearrange("p (n t) -> p t n", n=TS),
                              a_hi[:, :, TP:T].bitcast(f32), ALU.subtract).then_inc(a_ready, 1)

            base = st.base + st.k
            PER = 2 * 10
            dve.wait_ge(pool_set, 4)
            with dve.Fori(0, NB) as i:
                st.at(base + PER * i)
                for u in range(2):
                    q = Q_CONV + 6 * i + 3 * u
                    m = M_CONV + 6 * i + 3 * u
                    j2 = 2 * i + u
                    if u == 0:
                        dve.wait_ge(mask_ready, 16 * i + 16)
                    for n, j in enumerate((1, 2, 3, 0)):
                        g, th = j // 2, j % 2
                        wait_alone(dve, s_ready, 8 * i + (4 * u + n + 1))
                        for v in range(2):
                            h = 4 * g + 2 * th + v
                            ins = dve.tensor_tensor_reduce(
                                s_sb[:, h, :], bank[j][:, v * 256:(v + 1) * 256], mask_blk[:, :],
                                SCALE, -3.0e38, ALU.add, ALU.max, small[:, 0, h:h + 1])
                    st.done(ins)
                    st.wait()
                    sk = sinkp[:, 8 * u:8 * u + 8]
                    st.done(dve.tensor_tensor(small[:, 0, 0:8], small[:, 0, 0:8], sk, ALU.max))
                    st.wait()
                    st.done(dve.tensor_scalar(small[:, 1, 0:8], small[:, 0, 0:8], -1.0, None, ALU.mult))
                    dve.tensor_tensor(small[:, 2, 0:8], sk, small[:, 0, 0:8], ALU.subtract)\
                       .then_inc(m_ready, 1)
                    lo(q + 1)
                    complete(q)
                    scaled(c_sb[:, :], (3 * u) % 2, rstd2).then_inc(acc_free, 1)
                    dve.wait_ge(e_ready, j2 + 1)
                    st.done(dve.tensor_tensor(small[:, 3, 0:8], small[:, 3, 0:8], small[:, 4, 0:8],
                                              ALU.add))
                    st.wait()
                    st.done(dve.reciprocal(small[:, 5, 0:8], small[:, 3, 0:8]))
                    st.wait()
                    dve.tensor_tensor(s_sb[:, :, :], s_sb[:, :, :],
                                      small[:, 5, 0:8].unsqueeze(2).to_broadcast([P, 8, 2 * BLK]),
                                      ALU.mult).then_inc(prob_ready, 1)
                    lo(q + 2)
                    complete(q + 1)
                    dve.wait_ge(acc_free, m + 1)
                    scaled(zb[:, 2:T + 2], (3 * u + 1) % 2, c_sb).then_inc(acc_free, 1)
                    dve.wait_ge(acc_free, m + 2)
                    st.done(dve.tensor_scalar(cv[:, 0:TP], zb[:, 0:TP],
                                              chan[:, ds(C_CONVW + j2, 1)], None, ALU.mult))
                    st.wait()
                    st.done(dve.scalar_tensor_tensor(out=cv[:, 0:TP], in0=zb[:, 1:TP + 1],
                                                     scalar=chan[:, ds(C_CONVW + KA + j2, 1)],
                                                     in1=cv[:, 0:TP], op0=ALU.mult, op1=ALU.add))
                    st.wait()
                    st.done(dve.scalar_tensor_tensor(out=cv[:, 0:TP], in0=zb[:, 2:TP + 2],
                                                     scalar=chan[:, ds(C_CONVW + 2 * KA + j2, 1)],
                                                     in1=cv[:, 0:TP], op0=ALU.mult, op1=ALU.add))
                    st.done(dve.scalar_tensor_tensor(out=cv[:, TP:T], in0=zb[:, TP + 2:T + 2],
                                                     scalar=chan[:, ds(C_CONVW + 2 * KA + j2, 1)],
                                                     in1=row(cs_s, j2), op0=ALU.mult, op1=ALU.add))
                    dve.tensor_copy(row(ctail, j2), zb[:, TP:T + 2])
                    st.wait()
                    st.done(dve.tensor_tensor(cv[:, :], cv[:, :], rstd[:, :], ALU.mult))
                    for j in range(2):
                        dve.wait_ge(pT_ready, 8 * i + (4 * u + j + 3))
                        dve.tensor_copy(pT_sb[:, 2 + j, :], bank[2 + j]).then_inc(pT_dve, 1)
                    lo(q + 3)
                    complete(q + 2)
                    st.wait()
                    scaled(bt[:, :], (3 * u + 2) % 2, cv).then_inc(acc_free, 1)
                    dve.wait_ge(b_hi_ready, j2 + 1)
                    dve.tensor_tensor(row(b_lo, j2), bt[:, :], row(b_hi, j2).bitcast(f32),
                                      ALU.subtract).then_inc(b_ready, 1)
                    dve.wait_ge(a_hi_ready, j2 + 1)
                    dve.tensor_tensor(a_lo[:, 4 * u:4 * u + 4, ds(i * BLK, BLK)],
                                      bank[0].rearrange("p (t s) -> p t s", t=4),
                                      a_hi[:, 4 * u:4 * u + 4, ds(i * BLK, BLK)].bitcast(f32),
                                      ALU.subtract).then_inc(a_ready, 1)
                assert st.k == PER, st.k
            base += NB * PER

            with dve.Fori(0, KD) as i:
                q = Q_MERGE + 3 * i
                for j, gate in enumerate((ga_sb, gb_sb)):
                    lo(q + (1 + j))
                    complete(q + j)
                    scaled(gate[:, :], j).then_inc(acc_free, 1)
                for j, (gate, part) in enumerate(((ga_sb, ma_sb), (gb_sb, mb_sb))):
                    lo(q + 3, range(2 * j, 2 * j + 2))
                    dve.wait_ge(gate_out, 2 * i + (j + 1))
                    dve.wait_ge(w_used, 4 * q + (10 + 2 * j))
                    scaled(part[:, :], j, gate).then_inc(acc_free, 1)
                dve.wait_ge(acc_free, M_MERGE + 4 * i + 4)
                dve.tensor_tensor(row(merged, i), ma_sb[:, :], mb_sb[:, :], ALU.add)\
                   .then_inc(merged_ready, 1)
            with dve.Fori(0, KD) as k:
                dve.wait_ge(rhs_hi, k + (KD + 1))
                dve.tensor_tensor(row(h_lo, k), row(merged, k), row(h_hi, k).bitcast(f32),
                                  ALU.subtract).then_inc(rhs_ready, 1)

            with dve.Fori(0, KD // 2) as i:
                for u in range(2):
                    m = 2 * i + u
                    lo(Q_O + 1 + m)
                    complete(Q_O + m)
                    dve.tensor_copy(two(row(y_sb, m)), both(u)).then_inc(acc_free, 1)
            st.at(base)
            invert(1)
            base += 1
            dve.wait_ge(rstd_ready, 2)
            dve.wait_ge(x_back, 16)

            def new_x(i, count, gain):
                for u in range(2):
                    st.done(dve.scalar_tensor_tensor(out=tt[u][:, :], in0=row(y_sb, 2 * i + u),
                                                     scalar=chan[:, ds(gain + 2 * i + u, 1)],
                                                     in1=rstd[:, :], op0=ALU.mult, op1=ALU.mult))
                st.wait()
                for u in range(2):
                    dve.tensor_tensor(row(x_sb, 2 * i + u), row(x_sb, 2 * i + u), tt[u][:, :],
                                      ALU.add).then_inc(x_new, 1)
            with dve.Fori(0, KD // 2) as i:
                st.at(base + 2 * i)
                new_x(i, 0, C_MIXPOST)
                for u in range(2):
                    h_low(2 * i + u, C_FFNPRE, 2 * i + (2 * KD + 1 + u))
            base += KD
            st.at(base)
            invert(2)
            base += 1
            for k in range(KP):
                dve.wait_ge(p_split_hi, k + 1)
                dve.tensor_tensor(p_lo[:, k, :], p_raw[:, k, :], p_hi[:, k, :].bitcast(f32),
                                  ALU.subtract).then_inc(p_split, 1)
            dve.wait_ge(rstd_ready, 3)
            dve.wait_ge(pool_set, 5)
            dve.wait_ge(y_clear, 1)

            PERT = 5
            with dve.Fori(0, NCH) as c:
                with dve.Fori(0, CH) as t:
                    q = Q_FFN + Q_CHUNK * c + 2 * t
                    tile = CH * c + t
                    st.at(base + PERT * tile)
                    lo(q + 1)
                    complete(q)
                    scaled(fzb[:, 2:T + 2], 0).then_inc(acc_free, 1)
                    dve.wait_ge(acc_free, M_FFN + M_CHUNK * c + 2 * t + 1)
                    st.done(dve.tensor_scalar(fcv[:, 0:TP], fzb[:, 0:TP],
                                              chan[:, ds(C_FCONVW + tile, 1)], None, ALU.mult))
                    st.wait()
                    st.done(dve.scalar_tensor_tensor(out=fcv[:, 0:TP], in0=fzb[:, 1:TP + 1],
                                                     scalar=chan[:, ds(C_FCONVW + KF + tile, 1)],
                                                     in1=fcv[:, 0:TP], op0=ALU.mult, op1=ALU.add))
                    st.wait()
                    st.done(dve.scalar_tensor_tensor(out=fcv[:, TP:T], in0=fzb[:, TP + 2:T + 2],
                                                     scalar=chan[:, ds(C_FCONVW + 2 * KF + tile, 1)],
                                                     in1=row(fs_s, tile), op0=ALU.mult, op1=ALU.add))
                    dve.scalar_tensor_tensor(out=fcv[:, 0:TP], in0=fzb[:, 2:TP + 2],
                                             scalar=chan[:, ds(C_FCONVW + 2 * KF + tile, 1)],
                                             in1=fcv[:, 0:TP], op0=ALU.mult, op1=ALU.add)\
                       .then_inc(fconv_ready, 1)
                    st.done(dve.tensor_copy(row(ftail, tile), fzb[:, TP:T + 2]))
                    dve.wait_ge(gelu_ready, tile + 1)
                    st.done(dve.tensor_tensor(ge2[:, :], ge[:, :], rstd[:, :], ALU.mult))
                    lo(q + 2)
                    complete(q + 1)
                    st.wait()
                    scaled(ft[:, :], 1, ge2).then_inc(acc_free, 1)
                    dve.wait_ge(f_hi_ready, tile + 1)
                    dve.tensor_tensor(row(f_lo, t), ft[:, :], row(f_hi, t).bitcast(f32),
                                      ALU.subtract).then_inc(f_ready, 1)
                    assert st.k == PERT, st.k
                with dve.Fori(0, KD // 4) as j:
                    q = Q_FFN + Q_CHUNK * c + j + 2 * CH
                    for g in range(4):
                        dve.wait_ge(w_used, 4 * q + (g + 1))
                        yr = two(row(y_sb, 4 * j + g))
                        dve.tensor_tensor(yr, both(g % 2), yr, ALU.add).then_inc(acc_free, 1)
                        lo(q + 1, [g])
            base += PERT * KF

            def ple_evac(mt):
                if mt == 10:
                    dve.wait_ge(sq_added, 4 * KD + 1)
                if mt == 12:
                    dve.wait_ge(rstd_ready, 4)
                if mt % 2 == 0:
                    dve.wait_ge(ple_done, mt // 2 + 1)
                else:
                    dve.wait_ge(w_used, 4 * Q_PLE + (mt + 1) // 2)
                dve.tensor_copy(two(ple_sb[:, mt, :]), both((0, 1, 3)[mt % 3])).then_inc(ple_free, 1)
            for mt in range(12):
                if mt == 6:
                    lo(Q_PLE + 1, range(0, 2))
                if mt == 10:
                    lo(Q_PLE + 1, range(2, 4))
                ple_evac(mt)
            st.at(base)
            invert(3)
            base += 1
            for mt in range(12, KD):
                ple_evac(mt)
            lo(Q_GATE)
            with dve.Fori(0, KD // 2) as i:
                st.at(base + 2 * i)
                new_x(i, 0, C_FFNPOST)
                for u in range(2):
                    k = 2 * i + u
                    dve.wait_ge(rhs_hi, k + (3 * KD + 1))
                    dve.tensor_tensor(row(h_lo, k), row(x_sb, k), row(h_hi, k).bitcast(f32),
                                      ALU.subtract).then_inc(rhs_ready, 1)
            base += KD

            def gate(i, u, first=False, last=False):
                m = 2 * i + u
                if not last:
                    lo(Q_GATE + 1 + m)
                dve.wait_ge(acc_free, M_GATE + m + 1)
                if not first:
                    dve.wait_ge(x_out, m)
                dve.tensor_tensor(tt[1][:, :], tt[0][:, :], row(ple_sb, m), ALU.mult)\
                   .then_inc(sig_used, 1)
                dve.wait_ge(sig_used, m + 1)
                dve.tensor_tensor(row(x_sb, m), row(x_sb, m), tt[1][:, :], ALU.add)\
                   .then_inc(x_out, 1)
            gate(0, 0, first=True)
            gate(0, 1)
            with dve.Fori(1, KD // 2 - 1) as i:
                gate(i, 0)
                gate(i, 1)
            gate(KD // 2 - 1, 0)
            gate(KD // 2 - 1, 1, last=True)

        @block.gpsimd
        def _(pool):
            def row(t_, k):
                return t_[:, ds(k, 1), :].rearrange("p a t -> p (a t)")

            def add_squares(n, bufs, acc):
                with pool.Fori(0, KD // 2) as i:
                    for u in range(2):
                        pool.wait_ge(sq_ready, 16 * n + 2 * i + (u + 1))
                        pool.wait_ge(sq_added, 16 * n + 2 * i + (u + 1))
                        pool.tensor_tensor(acc[:, :], acc[:, :], bufs[u][:, :], ALU.add)\
                            .then_inc(sq_added, 1)

            pool.memset(sqacc1[:, :], 0.0).then_inc(sq_added, 1)
            pool.memset(kT_sb[:, 0:BLK], 0.0).then_inc(pool_set, 1)
            pool.memset(v_tok[:, 0, :], 0.0).then_inc(pool_set, 1)
            pool.memset(ones[:, :], 1.0).then_inc(pool_set, 1)
            pool.wait_ge(pool_set, 3)
            add_squares(0, sq_a, sqacc1)
            pool.memset(zb[:, 0:2], 0.0).then_inc(pool_set, 1)

            def cosine(r, src, dst):
                pool.wait_ge(acc_free, rope_tile(r))
                if not (isinstance(r, int) and r == 0):
                    pool.wait_ge(rope_done, r)
                pool.tensor_tensor(rope_c[:, :], src[:, :], cos[:, :], ALU.mult).then_inc(rope_cos, 1)
                pool.wait_ge(rope_cos, r + 1)
                pool.wait_ge(rope_sin, r + 1)
                pool.tensor_tensor(dst, rope_c[:, :], rope_s[:, :], ALU.add).then_inc(rope_done, 1)
            pool.wait_ge(tab_ready, 16 * 10)
            cosine(0, rope_in[0], kT_sb[:, BLK:BLK + T])
            pool.wait_ge(rope_done, 1)
            pool.dma_start(kT_out, kT_sb[:, TP:BLK + T]).then_inc(tail_out, 16)
            pool.wait_ge(acc_free, 2)
            pool.dma_start(vT_out, vT_sb[:, TP - BLK:T]).then_inc(tail_out, 16)
            pool.wait_ge(v_stored, 1)
            pool.dma_start(v_cache[0:1, :, :], v_new[:, :]).then_inc(v_placed, 16)
            with pool.Fori(0, KA // 2) as i:
                for u in range(2):
                    cosine(2 * i + (u + 1), rope_in[(u + 1) % 2], row(q_sb, 2 * i + u))

            pool.wait_ge(v_placed, 16)
            with pool.Fori(0, NB) as i:
                pool.wait_ge(a_ready, 2 * i + 1)
                pool.dma_start(mask_blk[:, :], mask_in[ds(i, 1), :, :].rearrange("a p n -> (a p) n"))\
                    .then_inc(mask_ready, 16)
                pool.tensor_copy(q_blk[:, :, :], q_sb[:, :, ds(i * BLK, BLK)]).then_inc(staged, 1)
                pool.tensor_copy(k_blk[:, :], kT_sb[:, ds(i * BLK, 2 * BLK)]).then_inc(staged, 1)
                pool.tensor_copy(v_blk[:, :, :], v_tok[:, ds(i, 2), :]).then_inc(staged, 1)

            pool.wait_ge(w_used, 4 * Q_O)
            pool.dma_start(x_sb[:, :, :], x_in).then_inc(x_back, 16)
            pool.wait_ge(merged_ready, KD)
            pool.memset(sqacc2[:, :], 0.0).then_inc(acc_zero, 1)
            pool.wait_ge(acc_zero, 1)
            add_squares(1, sq_b, sqacc2)
            pool.wait_ge(sum_ready, 2)
            pool.memset(sqacc2[:, :], 0.0).then_inc(acc_zero, 1)
            pool.wait_ge(acc_zero, 2)
            add_squares(2, sq_b, sqacc2)
            pool.dma_start(p_raw[:, :, :], p_in).then_inc(p_ready, 16)
            pool.memset(fzb[:, 0:2], 0.0).then_inc(pool_set, 1)
            pool.wait_ge(x_new, KD)
            pool.memset(y_sb[:, :, :], 0.0).then_inc(y_clear, 1)
            pool.wait_ge(p_split, KP)
            pool.memset(sqacc3[:, :], 0.0).then_inc(acc_zero, 1)
            pool.wait_ge(acc_zero, 3)
            add_squares(3, sq_c, sqacc3)
            pool.dma_start(ctail_out, ctail[:, :, :]).then_inc(tail_out, 16)
            pool.dma_start(ftail_out, ftail[:, :, :]).then_inc(tail_out, 16)
            with pool.Fori(0, KD) as m:
                pool.wait_ge(x_out, m + 1)
                pool.dma_start(y_out[ds(m, 1), :, :].rearrange("a p n -> (a p) n"), row(x_sb, m))\
                    .then_inc(out_done, 16)
            pool.wait_ge(out_done, 16 * KD)
            pool.wait_ge(tail_out, 16 * 4)


def _blocks(w, cols):
    k = w.shape[0] // P
    w = w[:, cols] if cols is not None else w
    return w.reshape(k, P, w.shape[1] // P, P).transpose(2, 0, 1, 3)


def _slots(blocks):
    n = blocks.reshape(-1, 4, P, P)
    return n.transpose(0, 2, 1, 3).reshape(-1, P, 4 * P)


def kernel(**inputs):
    import concourse.bacc as bacc
    from concourse.bass_utils import run_bass_kernel_spmd

    v = {n: np.asarray(a) for n, a in inputs.items()}
    f = np.float32
    pairs = np.concatenate([np.r_[HD * t:HD * t + HD, HD * (t + GRP):HD * (t + GRP) + HD]
                            for t in range(GRP)])
    w_in, up, down = v["w_in"][0], v["w_ffn_up"][0], v["w_ffn_down"][0]
    qw, kvw = w_in[:, 0:NH * HD], w_in[:, NH * HD:NH * HD + 2 * P]
    c0 = NH * HD + 2 * P
    cw = KA * P
    kv = _blocks(kvw, None)
    conv = np.stack([_blocks(w_in[:, c0 + o:c0 + o + cw], None) for o in (cw, 2 * cw, 0)], 1)
    ga = _blocks(w_in[:, c0 + 3 * cw:c0 + 3 * cw + D], None)
    gb = _blocks(w_in[:, c0 + 3 * cw + D:c0 + 3 * cw + 2 * D], None)
    br = np.concatenate([_blocks(v["w_attn_branch"][0][pairs], None),
                         _blocks(v["w_conv_branch"][0], None)], 1)
    merge = np.stack([ga, gb, br], 1)
    fa, fg = _blocks(up[:, :FF], None), _blocks(up[:, FF:], None)
    fd = _blocks(down, None)
    stream = [_slots(kv), _slots(_blocks(qw, pairs)), _slots(conv), _slots(merge),
              _slots(_blocks(v["w_o"][0], None))]
    for c in range(NCH):
        s = slice(CH * c, CH * c + CH)
        stream += [_slots(np.stack([fa[s], fg[s]], 1)), _slots(fd[:, s])]
    stream += [_slots(_blocks(v["w_ple"][0], None)), _slots(_blocks(v["w_ple_gate"][0], None))]
    wstream = np.concatenate(stream).reshape(NQ, 4, P, 4 * P)

    def fmajor(a):
        return a.T.reshape(a.shape[1] // P, P, a.shape[0]).transpose(1, 0, 2)

    def cols(a):
        return a.reshape(a.shape[0], -1, P).transpose(2, 0, 1).reshape(P, -1)
    x = fmajor(np.concatenate([v["x_prompt"][0], v["x_sample"][:, 0]]))
    p = fmajor(np.concatenate([v["p_prompt"][0, 0], v["p_sample"][0, :, 0]]))
    chan = np.concatenate([cols(v["norm_mix_pre"]), cols(v["norm_mix_post"]),
                           cols(v["norm_ffn_pre"]), cols(v["norm_ffn_post"]),
                           cols(v["conv_w"][0]), cols(v["b_gate"][0]),
                           cols(v["ffn_conv_w"][0]), cols(v["ffn_conv_b"])], 1)
    sk = v["attn_sinks"][0].reshape(NKV, 2, 4)
    sinkp = np.broadcast_to(sk.transpose(1, 0, 2).reshape(1, NH), (P, NH))
    sinks = np.repeat(v["attn_sinks"][0].reshape(NKV, GRP).T[:, :, None], TS, 2).reshape(GRP, -1)

    def state(a, k):
        return a.reshape(TS, 2, k, P).transpose(3, 2, 0, 1)
    ks = v["state_attn_k"][0].reshape(TS, BLK, P)
    vs = v["state_attn_v"][0].reshape(TS, BLK, P)
    eye = np.eye(P, dtype=f)
    rot = np.zeros((P, P), f)
    for h in range(2):
        for d in range(HD // 2):
            rot[HD * h + HD // 2 + d, HD * h + d] = -1.0
            rot[HD * h + d, HD * h + HD // 2 + d] = 1.0
    inv = (f(10000.0) ** (-np.arange(HD // 2, dtype=f) / f(HD // 2))).astype(f)
    pos = np.concatenate([np.arange(TP), np.full(TS, 2048)]).astype(f)
    ang = (pos[None, :] * inv[:, None]).astype(f)
    rots = np.stack([np.tile(np.cos(ang), (4, 1)), np.tile(np.sin(ang), (4, 1))]).astype(f)
    qi, ci = np.arange(BLK)[:, None], np.arange(2 * BLK)[None, :]
    rel = BLK + qi - ci
    band = (rel >= 0) & (rel < BLK)
    mask = np.stack([np.where(band & ((b > 0) | (ci >= BLK)), 0.0, -1e30) for b in range(NB)])

    feeds = dict(
        wstream=wstream, x=x, p=p, chan=chan, sinkp=sinkp, sinks=sinks,
        cstate=state(v["state_conv"][0], KA), fstate=state(v["state_ffn_conv"][0], KF),
        kcache=ks[:, 1:].transpose(2, 0, 1), vcache=vs[:, 1:].transpose(1, 0, 2),
        kstate=ks[:, 1:], vstate=vs[:, 1:],
        cst1=v["state_conv"][0][:, 1], fst1=v["state_ffn_conv"][0][:, 1],
        mats=np.stack([eye, rot]), rots=rots, mask=mask.astype(f))
    outs = dict(y=(KD, P, T), kT=(P, BLK + TS), vT=(P, BLK + TS), ctail=(P, KA, TS + 2),
                ftail=(P, KF, TS + 2), kold=(TS, BLK - 1, P), vold=(TS, BLK - 1, P),
                cold=(TS, KA * P), fold=(TS, FF))

    nc = bacc.Bacc("TRN2", target_bir_lowering=False, num_devices=1)
    arrays, args = {}, []
    for name, a in feeds.items():
        arrays[f"in_{name}"] = np.ascontiguousarray(a)
        args.append(nc.dram_tensor(f"in_{name}", list(a.shape), mybir.dt.from_np(a.dtype),
                                   kind="ExternalInput").ap())
    for name, shape in outs.items():
        args.append(nc.dram_tensor(f"out_{name}", list(shape), mybir.dt.float32,
                                   kind="ExternalOutput").ap())
    build(nc, *args)
    r = run_bass_kernel_spmd(nc, [arrays], core_ids=[0]).results[0]
    g = {n: np.asarray(r[f"out_{n}"]) for n in outs}

    def tmajor(a):
        return a.transpose(2, 1, 0).reshape(a.shape[2], -1)
    y = g["y"].reshape(D, T).T
    kt, vt = g["kT"].T, g["vT"].T
    ct, ft = tmajor(g["ctail"]), tmajor(g["ftail"])

    def new_state(old, new):
        return np.concatenate([old, new], 1)
    kn, vn = (new_state(o, t[BLK:, None]).reshape(1, TS, BLK, NKV, HD)
              for o, t in ((g["kold"], kt), (g["vold"], vt)))
    cn, fn = (new_state(o[:, None], t[2:, None])[None] for o, t in ((g["cold"], ct), (g["fold"], ft)))
    c = np.ascontiguousarray
    return (c(y[:TP])[None], c(y[TP:])[:, None],
            c(kt[:BLK]).reshape(1, 1, BLK, NKV, HD), c(vt[:BLK]).reshape(1, 1, BLK, NKV, HD),
            c(ct[:2])[None, None], c(ft[:2])[None, None], kn, vn, cn, fn)
```

```python
from contextlib import ExitStack

import concourse.bass as bass
from concourse import mybir
import numpy as np

P = 128
D = 2048
KD = D // P
TP, TS = 512, 8
T = TP + TS
HALF = T // 2
HD, NH, NKV, GRP = 64, 16, 2, 8
KA = NH * HD // P
FF = 5632
KF = FF // P
CH = 4
NCH = KF // CH
PLE = 256
KP = PLE // P
BLK = 128
NB = TP // BLK
EPS = 1e-6
SCALE = HD ** -0.5

Q_KV = 0
Q_Q = 2
Q_CONV = Q_Q + KA
Q_MERGE = Q_CONV + 3 * KA
Q_O = Q_MERGE + 3 * KD
Q_FFN = Q_O + KD
Q_CHUNK = 2 * CH + KD // 4
Q_PLE = Q_FFN + NCH * Q_CHUNK
Q_GATE = Q_PLE + 2
NQ = Q_GATE + KD
M_Q = 2
M_CONV = M_Q + KA
M_MERGE = M_CONV + 3 * KA
M_O = M_MERGE + 4 * KD
M_FFN = M_O + KD
M_CHUNK = 2 * CH + KD
M_GATE = M_FFN + NCH * M_CHUNK
C_MIXPRE, C_MIXPOST, C_FFNPRE, C_FFNPOST = 0, KD, 2 * KD, 3 * KD
C_CONVW = 4 * KD
C_BGATE = C_CONVW + 3 * KA
C_FCONVW = C_BGATE + 2 * KD
C_FCONVB = C_FCONVW + 3 * KF
NCHAN = C_FCONVB + KF


def build(nc, wstream, x_in, p_in, chan_in, sinkp_in, sinks_in, cstate_in, fstate_in, kcache_in,
          vcache_in, kstate_in, vstate_in, cst1_in, fst1_in, mats_in, rot_in, mask_in,
          y_out, kT_out, vT_out, ctail_out, ftail_out, kold_out, vold_out, cold_out, fold_out):
    f32, f32r = mybir.dt.float32, mybir.dt.float32r
    ALU, ACT, AX = mybir.AluOpType, mybir.ActivationFunctionType, mybir.AxisListType
    ds = bass.ds

    with ExitStack() as ctx:
        arena_base = -(-nc.sbuf_base // 64) * 64
        top = [arena_base]

        def region(nbytes):
            at = top[0]
            top[0] += -(-nbytes // 64) * 64
            return at

        def at(name, shape, offset, dt=f32):
            return nc.alloc_sbuf_tensor_at(name, [shape[0], *shape[1:]], dt, offset=offset)

        XB = T * 4
        r_wraw, r_whi, r_wlo = (region(4 * 4 * P * 4) for _ in range(3))
        r_hhi, r_hlo = region(KD * XB), region(KD * XB)
        r1, r2, r3 = region(KD * XB), region(KD * XB), region(KD * XB)

        w_raw = at("w_raw", [P, 4, 4 * P], r_wraw)
        w_hi = at("w_hi", [P, 4, 4 * P], r_whi, f32r)
        w_lo = at("w_lo", [P, 4, 4 * P], r_wlo, f32r)
        h_hi = at("h_hi", [P, KD, T], r_hhi, f32r)
        h_lo = at("h_lo", [P, KD, T], r_hlo, f32r)
        x_sb = at("x_sb", [P, KD, T], r1)
        a_hi = at("a_hi", [P, KA, T], r1, f32r)
        a_lo = at("a_lo", [P, KA, T], r1 + KA * XB, f32r)
        q_sb = at("q_sb", [P, KA, T], r1 + KA * XB)
        b_hi = at("b_hi", [P, KA, T], r2, f32r)
        b_lo = at("b_lo", [P, KA, T], r2 + KA * XB, f32r)
        y_sb = at("y_sb", [P, KD, T], r2)
        o = [r2]

        def sub(name, shape, dt=f32):
            t_ = at(name, shape, o[0], dt)
            o[0] += -(-int(np.prod(shape[1:])) // 8) * 32
            return t_

        cos = sub("cos", [P, T])
        sin = sub("sin", [P, T])
        rope_in = [sub(f"rope_in{i}", [P, T]) for i in range(2)]
        rope_s = sub("rope_s", [P, T])
        rope_c = sub("rope_c", [P, T])
        vT_sb = sub("vT_sb", [P, T])
        k_cache = sub("k_cache", [P, TS, BLK])
        v_cache = sub("v_cache", [P, TS, P])
        assert o[0] <= r2 + KD * XB
        o[0] = r3
        SR = 3 * 32 + GRP
        ss_sb = sub("ss_sb", [SR, TS // 2, BLK])
        pTs_sb = sub("pTs_sb", [P, TS // 2, SR])
        v_new = sub("v_new", [TS, P])
        cst_tmp = sub("cst_tmp", [P, KF, TS])
        cst_sb = sub("cst_sb", [P, KA, TS, 2])
        fst_sb = sub("fst_sb", [P, KF, TS, 2])
        assert o[0] <= r3 + KD * XB
        o[0] = r3
        s_sb = sub("s_sb", [P, 8, 2 * BLK])
        pT_sb = sub("pT_sb", [P, 4, 4 * BLK])
        q_blk = sub("q_blk", [P, KA, BLK])
        k_blk = sub("k_blk", [P, 2 * BLK])
        v_blk = sub("v_blk", [P, 2, P])
        mask_blk = sub("mask_blk", [P, 2 * BLK])
        c_sb = sub("c_sb", [P, T])
        zb = sub("zb", [P, T + 2])
        cv = sub("cv", [P, T])
        bt = sub("bt", [P, T])
        assert o[0] <= r3 + KD * XB, (o[0] - r3, KD * XB)
        merged = at("merged", [P, KD, T], r3)
        f_hi = at("f_hi", [P, CH, T], r3, f32r)
        f_lo = at("f_lo", [P, CH, T], r3 + CH * XB, f32r)
        o[0] = r3 + 2 * CH * XB
        fzb = sub("fzb", [P, T + 2])
        fcv = sub("fcv", [P, T])
        ge = sub("ge", [P, T])
        ge2 = sub("ge2", [P, T])
        ft = sub("ft", [P, T])
        p_raw = sub("p_raw", [P, KP, T])
        assert o[0] <= r3 + KD * XB
        ple_sb = at("ple_sb", [P, KD, T], r3)
        o[0] = top[0]
        chan = sub("chan", [P, NCHAN])
        ident = sub("ident", [P, P])
        rotm = sub("rotm", [P, P])
        ones = sub("ones", [P, P])
        rstd = sub("rstd", [P, T])
        sinkp = sub("sinkp", [P, NH])
        sinks = sub("sinks", [P, 1])
        cs_s = sub("cs_s", [P, KA, TS])
        fs_s = sub("fs_s", [P, KF, TS])
        ctail = sub("ctail", [P, KA, TS + 2])
        ftail = sub("ftail", [P, KF, TS + 2])
        small = sub("small", [P, 6, 8])
        table_out = sub("table_out", [P, 1])
        t0 = o[0]
        kT_sb = sub("kT_sb", [P, BLK + T])
        v_tok = sub("v_tok", [P, NB + 1, P])
        rstd2 = sub("rstd2", [P, T])
        sqacc1 = sub("sqacc1", [P, T])
        end = o[0]
        o[0] = t0
        ga_sb = sub("ga_sb", [P, T])
        gb_sb = sub("gb_sb", [P, T])
        ma_sb = sub("ma_sb", [P, T])
        mb_sb = sub("mb_sb", [P, T])
        end = max(end, o[0])
        o[0] = t0
        p_hi = sub("p_hi", [P, KP, T], f32r)
        p_lo = sub("p_lo", [P, KP, T], f32r)
        tt = [sub(f"tt{i}", [P, T]) for i in range(2)]
        end = max(end, o[0])
        sq_a = [at(f"sq_a{i}", [P, T], r3 + (14 + i) * XB) for i in range(2)]
        nv_a = at("nv_a", [P, T], r3 + 13 * XB)
        sq_b = [at(f"sq_b{i}", [P, T], t0 + i * XB) for i in range(2)]
        sqacc2 = at("sqacc2", [P, T], t0 + 2 * XB)
        nv_b = at("nv_b", [P, T], t0 + 3 * XB)
        sq_c = [at(f"sq_c{i}", [P, T], r3 + (10 + i) * XB) for i in range(2)]
        nv_c = at("nv_c", [P, T], r3 + 13 * XB)
        sqacc3 = at("sqacc3", [P, T], r3 + 14 * XB)
        assert end <= nc.sbuf_usable_end, (end, nc.sbuf_usable_end)

        pair = [ctx.enter_context(nc.psum_tensor(f"pair{i}", [P, 2, 512], f32)) for i in range(4)]
        bank = [pair[2][:, 0, :], pair[2][:, 1, :], pair[3][:, 0, :], pair[3][:, 1, :]]

        def both(i):
            return pair[i][:, :, 0:HALF]

        def two(ap):
            return ap.rearrange("p (h t) -> p h t", h=2)

        def row(t_, k):
            return t_[:, ds(k, 1), :].rearrange("p a t -> p (a t)")

        def sem(name):
            return ctx.enter_context(nc.semaphore(name))

        raw_ready = [sem(f"raw_ready{g}") for g in range(4)]
        hi_ready = sem("hi_ready")
        lo_ready = sem("lo_ready")
        w_used = sem("w_used")
        acc_free = sem("acc_free")
        X_PARTS = ((0, 1), (1, 2), (2, 4), (4, 8), (8, 12), (12, 16))
        in_ready = [sem(f"in_ready{i}") for i in range(len(X_PARTS))]
        chan_ready = sem("chan_ready")
        tab_ready = sem("tab_ready")
        x_back = sem("x_back")
        p_ready = sem("p_ready")
        mask_ready = sem("mask_ready")
        rhs_hi = sem("rhs_hi")
        rhs_ready = sem("rhs_ready")
        sq_ready = sem("sq_ready")
        sq_added = sem("sq_added")
        acc_zero = sem("acc_zero")
        sum_ready = sem("sum_ready")
        xsq_ready = sem("xsq_ready")
        xsq_summed = sem("xsq_summed")
        xy_ready = sem("xy_ready")
        inv_ready = sem("inv_ready")
        rstd_ready = sem("rstd_ready")
        dve_step = sem("dve_step")
        pool_set = sem("pool_set")
        rope_rot = sem("rope_rot")
        rope_sin = sem("rope_sin")
        rope_cos = sem("rope_cos")
        rope_done = sem("rope_done")
        v_turned = sem("v_turned")
        v_stored = sem("v_stored")
        v_placed = sem("v_placed")
        k_placed = sem("k_placed")
        ss_ready = sem("ss_ready")
        ss_scaled = sem("ss_scaled")
        ss_shift = sem("ss_shift")
        ss_exp = sem("ss_exp")
        ss_prob = sem("ss_prob")
        ss_turned = sem("ss_turned")
        ss_copied = sem("ss_copied")
        ss_out = sem("ss_out")
        ss_hi = sem("ss_hi")
        staged_qk = sem("staged_qk")
        staged_v = sem("staged_v")
        s_ready = sem("s_ready")
        m_ready = sem("m_ready")
        e_ready = sem("e_ready")
        prob_ready = sem("prob_ready")
        pT_ready = sem("pT_ready")
        pT_act = sem("pT_act")
        pT_dve = sem("pT_dve")
        pv_ready = sem("pv_ready")
        a_hi_ready = sem("a_hi_ready")
        a_ready = sem("a_ready")
        b_hi_ready = sem("b_hi_ready")
        b_ready = sem("b_ready")
        gate_out = sem("gate_out")
        merged_ready = sem("merged_ready")
        y_clear = sem("y_clear")
        x_new = sem("x_new")
        p_split_hi = sem("p_split_hi")
        p_split = sem("p_split")
        fconv_ready = sem("fconv_ready")
        gelu_ready = sem("gelu_ready")
        f_hi_ready = sem("f_hi_ready")
        f_ready = sem("f_ready")
        ple_free = sem("ple_free")
        ple_done = sem("ple_done")
        sig_used = sem("sig_used")
        x_out = sem("x_out")
        out_done = sem("out_done")
        copy_done = sem("copy_done")
        tail_out = sem("tail_out")

        def rope_tile(r):
            return 1 if isinstance(r, int) and r == 0 else M_Q + r

        passed = sem("passed")

        def wait_alone(eng, semaphore, value):
            eng.wait_ge(semaphore, value)
            eng.sem_inc(passed, 1)

        block = ctx.enter_context(nc.Block())

        @block.sync
        def _(sp):
            sp.dma_start(chan[:, :], chan_in).then_inc(chan_ready, 16)
            for g in range(4):
                sp.dma_start(w_raw[:, g, :], wstream[0, g, :, :]).then_inc(raw_ready[g], 16)
                for part, (k0, k1) in enumerate(X_PARTS):
                    if k0 // 4 == g:
                        sp.dma_start(x_sb[:, k0:k1, :], x_in[:, k0:k1, :])\
                          .then_inc(in_ready[part], 16)
            for dst, src in ((ident[:, :], mats_in[0, :, :]), (rotm[:, :], mats_in[1, :, :]),
                             (cos[:, :], rot_in[0, :, :]), (sin[:, :], rot_in[1, :, :]),
                             (sinkp[:, :], sinkp_in), (sinks[:, :], sinks_in),
                             (k_cache[:, :, 1:BLK], kcache_in), (v_cache[1:BLK, :, :], vcache_in),
                             (cst_sb[:, :, :, :], cstate_in), (fst_sb[:, :, :, :], fstate_in)):
                sp.dma_start(dst, src).then_inc(tab_ready, 16)
            for dst, src in ((kold_out, kstate_in), (vold_out, vstate_in),
                             (cold_out, cst1_in), (fold_out, fst1_in)):
                sp.dma_start(dst, src).then_inc(copy_done, 16)
            with sp.Fori(1, NQ) as q:
                for g in range(4):
                    sp.wait_ge(lo_ready, 4 * q + (g - 3))
                    sp.dma_start(w_raw[:, g, :],
                                 wstream[ds(q, 1), g, :, :].rearrange("a p n -> (a p) n"))\
                      .then_inc(raw_ready[g], 16)
            sp.wait_ge(copy_done, 64)

        @block.tensor
        def _(pe):
            def products(acc, slot, kk, rhi, rlo, k, start, stop):
                w = slice(kk * P, kk * P + P)
                for wt, r, first, last in ((w_hi, rhi, True, False), (w_hi, rlo, False, False),
                                           (w_lo, rhi, False, True)):
                    for h in range(2):
                        mm = pe.matmul(pair[acc][:, h, 0:HALF], wt[:, slot, w],
                                       r[:, k, h * HALF:(h + 1) * HALF],
                                       start=start and first, stop=stop and last)
                return mm

            def d_tile(q, m, acc, rows, wait_rows=True, rhi=h_hi, rlo=h_lo, between={}):
                if not (isinstance(m, int) and m < 2):
                    pe.wait_ge(acc_free, m - 1)
                for g in range(4):
                    pe.wait_ge(lo_ready, 4 * q + (g + 1))
                    for kk in range(4):
                        if wait_rows:
                            if isinstance(q, int):
                                pe.wait_ge(rhs_ready, rows + 4 * g + kk + 1)
                            elif kk == 0:
                                pe.wait_ge(rhs_ready, rows + 4 * g + 4)
                        mm = products(acc, g, kk, rhi, rlo, 4 * g + kk,
                                      g == 0 and kk == 0, g == 3 and kk == 3)
                    mm.then_inc(w_used, 1)
                    if g in between:
                        between[g]()

            def feature_sum(n, sqacc):
                pe.wait_ge(sq_added, 16 * n + 17)
                for h in range(2):
                    mm = pe.matmul(pair[2][:, h, 0:HALF], ones[:, :],
                                   sqacc[:, h * HALF:(h + 1) * HALF], start=True, stop=True)
                mm.then_inc(sum_ready, 1)

            def rotate(r, src):
                pe.wait_ge(acc_free, rope_tile(r))
                if not (isinstance(r, int) and r == 0):
                    pe.wait_ge(rope_sin, r)
                for h in range(2):
                    mm = pe.matmul(pair[3][:, h, 0:HALF], rotm[:, :],
                                   src[:, h * HALF:(h + 1) * HALF], start=True, stop=True)
                mm.then_inc(rope_rot, 1)

            d_tile(0, 0, 0, 0)
            pe.wait_ge(pool_set, 3)
            feature_sum(0, sqacc1)
            d_tile(1, 1, 1, 0, wait_rows=False)
            pe.wait_ge(tab_ready, 16 * 10)
            rotate(0, rope_in[0])
            pe.wait_ge(acc_free, 2)
            pe.wait_ge(inv_ready, 1)
            for b in range(NB):
                pe.transpose(bank[0][:, b * P:(b + 1) * P], vT_sb[:, b * P:(b + 1) * P], ident[:, :])
            pe.transpose(bank[1][0:TS, 0:P], vT_sb[:, TP:T], ident[:, :]).then_inc(v_turned, 1)

            def q_pair(i, first):
                for u in range(2):
                    t = 2 * i + u
                    d_tile(Q_Q + t, M_Q + t, u, 0, wait_rows=False)
                    if not (first and u == 0):
                        rotate(t, rope_in[u])
            q_pair(0, True)
            with pe.Fori(1, KA // 2) as i:
                q_pair(i, False)
            def sample_scores():
                pe.wait_ge(rope_done, KA + 1)
                pe.wait_ge(k_placed, 1)
                pe.wait_ge(v_stored, 1)
                pe.wait_ge(rope_sin, KA + 1)
                for g in range(NKV):
                    for n in range(TS):
                        r = 32 * (2 * g + n % 2)
                        mm = pe.matmul(bank[2 * g][r:r + GRP, (n // 2) * P:(n // 2 + 1) * P],
                                       q_sb[HD * g:HD * g + HD, :, TP + n],
                                       k_cache[HD * g:HD * g + HD, n, :], start=True, stop=True)
                    mm.then_inc(ss_ready, 1)

            def sample_turn():
                pe.wait_ge(ss_prob, 1)
                for n in range(TS // 2):
                    mm = pe.transpose(bank[1][:, n * SR:(n + 1) * SR], ss_sb[:, n, :],
                                      ident[0:SR, 0:SR])
                mm.then_inc(ss_turned, 1)

            def sample_values():
                pe.wait_ge(ss_copied, 1)
                pe.wait_ge(v_placed, 16)
                for g in range(NKV):
                    for n in range(TS):
                        r = 32 * (2 * g + n % 2)
                        mm = pe.matmul(bank[0][HD * g:HD * g + HD, n * TS:(n + 1) * TS],
                                       v_cache[:, n, HD * g:HD * g + HD], pTs_sb[:, n // 2, r:r + GRP],
                                       start=True, stop=True)
                mm.then_inc(ss_out, 1)

            def scores(i, u):
                pe.wait_ge(staged_qk, 2 * i + 2)
                for j in (1, 2, 3, 0):
                    if j == 0:
                        pe.wait_ge(a_ready, 2 * i + (u + 1))
                    g, th = j // 2, j % 2
                    for v in range(2):
                        mm = pe.matmul(bank[j][:, v * 256:(v + 1) * 256],
                                       q_blk[HD * g:HD * g + HD, 4 * u + 2 * th + v, :],
                                       k_blk[HD * g:HD * g + HD, :], start=True, stop=True)
                    mm.then_inc(s_ready, 1)

            def turn(i, u):
                pe.wait_ge(prob_ready, 2 * i + (u + 1))
                for g in range(NKV):
                    for j in range(2):
                        for t in range(4):
                            mm = pe.transpose(bank[2 * g + j][:, t * P:(t + 1) * P],
                                              s_sb[:, 4 * g + t, j * P:(j + 1) * P],
                                              ident[:, :])
                        mm.then_inc(pT_ready, 1)

            def values(i, u):
                pe.wait_ge(staged_v, i + 1)
                pe.wait_ge(pT_act, 4 * i + (2 * u + 2))
                pe.wait_ge(pT_dve, 4 * i + (2 * u + 2))
                for g in range(NKV):
                    for j in range(2):
                        mm = pe.matmul(bank[0][HD * g:HD * g + HD, :],
                                       v_blk[:, j, HD * g:HD * g + HD],
                                       pT_sb[:, 2 * g + j, :], start=(j == 0), stop=(j == 1))
                mm.then_inc(pv_ready, 1)

            d_tile(Q_CONV, M_CONV, 0, 0, wait_rows=False,
                   between={0: lambda: rotate(KA, rope_in[KA % 2]), 2: sample_scores})
            d_tile(Q_CONV + 1, M_CONV + 1, 1, 0, wait_rows=False,
                   between={1: sample_turn, 2: sample_values})
            scores(0, 0)
            d_tile(Q_CONV + 2, M_CONV + 2, 0, 0, wait_rows=False)
            turn(0, 0)
            values(0, 0)

            def half_block(i, u):
                q = Q_CONV + 6 * i + 3 * u
                m = M_CONV + 6 * i + 3 * u
                scores(i, u)
                d_tile(q, m, (3 * u) % 2, 0, wait_rows=False)
                d_tile(q + 1, m + 1, (3 * u + 1) % 2, 0, wait_rows=False)
                turn(i, u)
                d_tile(q + 2, m + 2, (3 * u + 2) % 2, 0, wait_rows=False)
                values(i, u)
            half_block(0, 1)
            with pe.Fori(1, NB) as i:
                half_block(i, 0)
                half_block(i, 1)

            with pe.Fori(0, KD) as i:
                q = Q_MERGE + 3 * i
                m = M_MERGE + 4 * i
                d_tile(q, m, 0, 0, wait_rows=False)
                d_tile(q + 1, m + 1, 1, 0, wait_rows=False)
                for half, (rhi, rlo, ready, n) in enumerate(
                        ((a_hi, a_lo, a_ready, 2 * NB + 1), (b_hi, b_lo, b_ready, KA))):
                    pe.wait_ge(acc_free, m + (1 + half))
                    pe.wait_ge(ready, n)
                    for g in range(2):
                        pe.wait_ge(lo_ready, 4 * q + (9 + 2 * half + g))
                        for kk in range(4):
                            mm = products(half, 2 * half + g, kk, rhi, rlo, 4 * g + kk,
                                          g == 0 and kk == 0, g == 1 and kk == 3)
                        mm.then_inc(w_used, 1)

            with pe.Fori(0, KD // 2) as i:
                for u in range(2):
                    d_tile(Q_O + 2 * i + u, M_O + 2 * i + u, u, KD)
            feature_sum(1, sqacc2)
            pe.wait_ge(inv_ready, 2)

            def up(c, t, us=range(2)):
                for u in us:
                    d_tile(Q_FFN + Q_CHUNK * c + 2 * t + u, M_FFN + M_CHUNK * c + 2 * t + u,
                           u, 2 * KD)

            def up_first():
                pe.wait_ge(acc_free, M_FFN - 1)
                for k in range(KD):
                    if k % 4 == 0:
                        pe.wait_ge(lo_ready, 4 * Q_FFN + k // 4 + 1)
                    pe.wait_ge(rhs_ready, 2 * KD + k + 1)
                    mm = products(0, k // 4, k % 4, h_hi, h_lo, k, k == 0, k == KD - 1)
                    if k % 4 == 3:
                        mm.then_inc(w_used, 1)
                    pe.wait_ge(xsq_ready, k + 1)
                    for h in range(2):
                        mm = pe.matmul(pair[2][:, h, 0:HALF], ones[:, :],
                                       sq_b[k % 2][:, h * HALF:(h + 1) * HALF],
                                       start=(k == 0), stop=(k == KD - 1))
                    mm.then_inc(xsq_summed, 1)

            def down(c):
                with pe.Fori(0, KD // 4) as j:
                    for g in range(4):
                        pe.wait_ge(acc_free, M_FFN + M_CHUNK * c + 4 * j + (2 * CH + g - 1))
                        pe.wait_ge(lo_ready, 4 * (Q_FFN + Q_CHUNK * c + j) + (8 * CH + g + 1))
                        for kk in range(CH):
                            if g == 0:
                                pe.wait_ge(f_ready, CH * c + (kk + 1))
                            mm = products(g % 2, g, kk, f_hi, f_lo, kk, kk == 0, kk == CH - 1)
                        mm.then_inc(w_used, 1)
            up_first()
            up(0, 0, [1])
            with pe.Fori(1, CH) as t:
                up(0, t)
            down(0)
            with pe.Fori(1, NCH) as c:
                with pe.Fori(0, CH) as t:
                    up(c, t)
                down(c)

            pe.wait_ge(acc_free, M_GATE)
            pe.wait_ge(p_split, KP)
            for mt in range(KD):
                acc = (0, 1, 3)[mt % 3]
                if mt == 3:
                    feature_sum(2, sqacc3)
                if mt >= 3:
                    pe.wait_ge(ple_free, mt - 2)
                if mt % 2 == 0:
                    pe.wait_ge(lo_ready, 4 * Q_PLE + mt // 2 + 1)
                for kk in range(KP):
                    mm = products(acc, (mt // 2) % 4, 2 * (mt % 2) + kk, p_hi, p_lo, kk,
                                  kk == 0, kk == KP - 1)
                mm.then_inc(w_used if mt % 2 else ple_done, 1)
            pe.wait_ge(ple_free, KD)
            def gate(i, u, wait_rows=False):
                d_tile(Q_GATE + 2 * i + u, M_GATE + 2 * i + u, u, 3 * KD, wait_rows=wait_rows)
            gate(0, 0, wait_rows=True)
            gate(0, 1)
            with pe.Fori(1, KD // 2) as i:
                gate(i, 0)
                gate(i, 1)

        @block.scalar
        def _(act):
            def hi(q, slots=range(4)):
                for g in slots:
                    act.wait_ge(raw_ready[g], 16 * q + 16)
                    if not (isinstance(q, int) and q == 0):
                        act.wait_ge(w_used, 4 * q + (g - 3))
                    nc.scalar.activation(w_hi[:, g, :], w_raw[:, g, :], ACT.Copy)\
                      .then_inc(hi_ready, 1)

            def root(n):
                act.wait_ge(inv_ready, n + 1)
                src = (nv_a, nv_b, nv_b, nv_c)[n]
                nc.scalar.activation(rstd[:, :], src[:, :], ACT.Sqrt).then_inc(rstd_ready, 1)

            def scale_square_x(k, u):
                nc.scalar.activation(row(h_hi, k), row(x_sb, k), ACT.Copy,
                                     scale=chan[:, ds(C_MIXPRE + k, 1)]).then_inc(rhs_hi, 1)
                if not (isinstance(k, int) and k < 2):
                    wait_alone(act, sq_added, k)
                nc.scalar.activation(sq_a[u][:, :], row(x_sb, k), ACT.Square).then_inc(sq_ready, 1)
            hi(0, [0])
            act.wait_ge(chan_ready, 16)
            for part, (k0, k1) in enumerate(X_PARTS):
                if part > 2:
                    hi(0, [k0 // 4])
                act.wait_ge(in_ready[part], 16)
                if k1 - k0 < 4:
                    for k in range(k0, k1):
                        scale_square_x(k, k % 2)
                else:
                    with act.Fori(0, 2) as i:
                        for u in range(2):
                            scale_square_x(k0 + 2 * i + u, u)
            hi(1)
            root(0)
            hi(2)
            with act.Fori(0, KA) as t:
                hi(Q_Q + 1 + t)
            hi(Q_CONV + 1, range(3))
            act.wait_ge(ss_ready, 2)
            act.wait_ge(pool_set, 5)
            for r in (64, 96):
                nc.scalar.activation(ss_sb[r:r + GRP, :, :],
                                     bank[2][r:r + GRP, :].rearrange("p (n s) -> p n s", n=TS // 2),
                                     ACT.Copy, scale=SCALE).then_inc(ss_scaled, 1)
            hi(Q_CONV + 1, [3])
            act.wait_ge(ss_shift, 2)
            nc.scalar.activation(ss_sb[:, :, :], ss_sb[:, :, :], ACT.Exp).then_inc(ss_exp, 1)
            nc.scalar.activation(small[0:SR, 2, 0:4], small[0:SR, 1, 0:4], ACT.Exp)\
              .then_inc(ss_exp, 1)
            hi(Q_CONV + 2)
            act.wait_ge(ss_out, 1)
            nc.scalar.activation(a_hi[:, :, TP:T],
                                 bank[0][:, 0:TS * GRP].rearrange("p (n t) -> p t n", n=TS),
                                 ACT.Copy).then_inc(ss_hi, 1)

            def exponentials(i, u):
                act.wait_ge(m_ready, 2 * i + (u + 1))
                for h in range(8):
                    nc.scalar.activation(s_sb[:, h, :], s_sb[:, h, :], ACT.Exp,
                                         bias=small[:, 1, h:h + 1],
                                         accum_out=small[:, 3, h:h + 1])
                nc.scalar.activation(small[:, 4, 0:8], small[:, 2, 0:8], ACT.Exp)\
                  .then_inc(e_ready, 1)

            def turned(i, u):
                for j in range(2):
                    act.wait_ge(pT_ready, 8 * i + (4 * u + j + 1))
                    nc.scalar.activation(pT_sb[:, j, :], bank[j], ACT.Copy).then_inc(pT_act, 1)

            def conv_out(i, u):
                wait_alone(act, acc_free, M_CONV + 6 * i + (3 * u + 3))
                nc.scalar.activation(row(b_hi, 2 * i + u), bt[:, :], ACT.Copy).then_inc(b_hi_ready, 1)

            def attention_out(i, u):
                wait_alone(act, pv_ready, 2 * i + (u + 1))
                nc.scalar.activation(a_hi[:, 4 * u:4 * u + 4, ds(i * BLK, BLK)],
                                     bank[0].rearrange("p (t s) -> p t s", t=4),
                                     ACT.Copy).then_inc(a_hi_ready, 1)

            def half_block(i, u):
                q = Q_CONV + 6 * i + 3 * u
                hi(q + 1)
                exponentials(i, u)
                hi(q + 2)
                turned(i, u)
                hi(q + 3)
                conv_out(i, u)
                attention_out(i, u)
            exponentials(0, 0)
            hi(Q_CONV + 3)
            conv_out(0, 0)
            turned(0, 0)
            attention_out(0, 0)
            half_block(0, 1)
            with act.Fori(1, NB) as i:
                half_block(i, 0)
                half_block(i, 1)

            def warm(func):
                nc.scalar.activation(table_out[:, :], chan[:, 0:1], func)

            def gates(i, then):
                q = Q_MERGE + 3 * i
                hi(q + 1)
                for j, gate in enumerate((ga_sb, gb_sb)):
                    wait_alone(act, acc_free, M_MERGE + 4 * i + (j + 1))
                    nc.scalar.activation(gate[:, :], gate[:, :], ACT.Sigmoid,
                                         bias=chan[:, ds(C_BGATE + KD * j + i, 1)])\
                      .then_inc(gate_out, 1)
                    if j == 0:
                        hi(q + 2)
                then(q)
            warm(ACT.Sigmoid)
            with act.Fori(0, KD - 1) as i:
                gates(i, lambda q: hi(q + 3))

            def split_merged(q):
                for g in range(4):
                    hi(q + 3, [g])
                    for k in range(4 * g, 4 * g + 4):
                        act.wait_ge(merged_ready, k + 1)
                        nc.scalar.activation(h_hi[:, k, :], merged[:, k, :], ACT.Copy)\
                          .then_inc(rhs_hi, 1)
            gates(KD - 1, split_merged)
            warm(ACT.Sqrt)

            with act.Fori(0, KD // 2) as i:
                for u in range(2):
                    m = 2 * i + u
                    hi(Q_O + 1 + m)
                    act.wait_ge(acc_free, M_O + m + 1)
                    wait_alone(act, sq_added, m + KD)
                    nc.scalar.activation(sq_b[u][:, :], row(y_sb, m), ACT.Square).then_inc(sq_ready, 1)
            root(1)
            def square_new_x(i, first):
                for u in range(2):
                    k = 2 * i + u
                    wait_alone(act, x_new, k + 1)
                    nc.scalar.activation(row(h_hi, k), row(x_sb, k), ACT.Copy,
                                         scale=chan[:, ds(C_FFNPRE + k, 1)]).then_inc(rhs_hi, 1)
                    if not first:
                        wait_alone(act, xsq_summed, k - 1)
                    nc.scalar.activation(sq_b[u][:, :], row(x_sb, k), ACT.Square).then_inc(xsq_ready, 1)
            square_new_x(0, True)
            with act.Fori(1, KD // 2) as i:
                square_new_x(i, False)

            def up(c, t, first=False):
                q = Q_FFN + Q_CHUNK * c + 2 * t
                hi(q + 1)
                if first:
                    root(2)
                wait_alone(act, fconv_ready, CH * c + t + 1)
                nc.scalar.activation(ge[:, :], fcv[:, :], ACT.Gelu_apprx_tanh,
                                     bias=chan[:, ds(C_FCONVB + CH * c + t, 1)])\
                  .then_inc(gelu_ready, 1)
                hi(q + 2, range(3))
                wait_alone(act, acc_free, M_FFN + M_CHUNK * c + 2 * t + 2)
                nc.scalar.activation(row(f_hi, t), ft[:, :], ACT.Copy).then_inc(f_hi_ready, 1)
                hi(q + 2, [3])

            def down(c, last=False):
                with act.Fori(0, KD // 4) as j:
                    for g in range(4):
                        hi(Q_FFN + Q_CHUNK * c + j + (2 * CH + 1), [g])
                        if last:
                            wait_alone(act, acc_free, M_GATE - KD + 1 + 4 * j + g)
                            wait_alone(act, sq_added, 2 * KD + 4 * j + g)
                            nc.scalar.activation(sq_c[g % 2][:, :], row(y_sb, 4 * j + g), ACT.Square).then_inc(sq_ready, 1)
            up(0, 0, first=True)
            with act.Fori(1, CH) as t:
                up(0, t)
            act.wait_ge(p_ready, 16)
            for k in range(KP):
                nc.scalar.activation(p_hi[:, k, :], p_raw[:, k, :], ACT.Copy).then_inc(p_split_hi, 1)
            down(0)
            with act.Fori(1, NCH - 1) as c:
                with act.Fori(0, CH) as t:
                    up(c, t)
                down(c)
            with act.Fori(0, CH) as t:
                up(NCH - 1, t)
            warm(ACT.Sqrt)
            down(NCH - 1, last=True)

            def ple_evac(mt):
                if mt == 10:
                    act.wait_ge(sq_added, 3 * KD + 1)
                if mt == 14:
                    act.wait_ge(sum_ready, 3)
                if mt % 2 == 0:
                    act.wait_ge(ple_done, mt // 2 + 1)
                else:
                    act.wait_ge(w_used, 4 * Q_PLE + (mt + 1) // 2)
                nc.scalar.activation(two(ple_sb[:, mt, :]), both((0, 1, 3)[mt % 3]), ACT.Copy)\
                  .then_inc(ple_free, 1)

            def x_hi(k):
                act.wait_ge(x_new, k + (KD + 1))
                nc.scalar.activation(h_hi[:, k, :], x_sb[:, k, :], ACT.Copy).then_inc(rhs_hi, 1)
            k = 0
            for mt in range(KD):
                ple_evac(mt)
                if mt == 3:
                    root(3)
                if mt % 2 == 1:
                    hi(Q_PLE + 1 if mt < 8 else Q_GATE, [mt // 2 % 4])
                if mt >= 5:
                    x_hi(k)
                    k += 1
            for k in range(k, KD):
                x_hi(k)
            warm(ACT.Sigmoid)

            def gate(i, u, first=False, last=False):
                m = 2 * i + u
                if not last:
                    hi(Q_GATE + 1 + m)
                act.wait_ge(w_used, 4 * (Q_GATE + m) + 4)
                if not first:
                    act.wait_ge(sig_used, m)
                nc.scalar.activation(two(tt[0][:, :]), both(u), ACT.Sigmoid)\
                  .then_inc(acc_free, 1)
            gate(0, 0, first=True)
            gate(0, 1)
            with act.Fori(1, KD // 2 - 1) as i:
                gate(i, 0)
                gate(i, 1)
            gate(KD // 2 - 1, 0)
            gate(KD // 2 - 1, 1, last=True)

        @block.vector
        def _(dve):
            class Steps:
                base, k = 0, 0

                def at(self, base):
                    self.base, self.k = base, 0

                def done(self, ins):
                    ins.then_inc(dve_step, 1)
                    self.k += 1

                def wait(self):
                    dve.wait_ge(dve_step, self.base + self.k)
            st = Steps()

            def lo(q, slots=range(4)):
                for g in slots:
                    dve.wait_ge(hi_ready, 4 * q + (g + 1))
                    dve.tensor_tensor(w_lo[:, g, :], w_raw[:, g, :], w_hi[:, g, :].bitcast(f32),
                                      ALU.subtract).then_inc(lo_ready, 1)

            def complete(q):
                dve.wait_ge(w_used, 4 * q + 4)

            def scaled(dst, acc, by=rstd):
                return dve.tensor_tensor(two(dst), both(acc), two(by[:, :]), ALU.mult)

            def invert(n):
                dst = (nv_a, nv_b, nv_b, nv_c)[n]
                if n == 2:
                    dve.wait_ge(xsq_summed, KD)
                    dve.wait_ge(rstd_ready, 2)
                else:
                    dve.wait_ge(sum_ready, (1, 2, None, 3)[n])
                st.done(dve.tensor_scalar(two(dst[:, :]), both(2), 1.0 / D, EPS, ALU.mult, ALU.add))
                st.wait()
                dve.reciprocal(dst[:, :], dst[:, :]).then_inc(inv_ready, 1)

            def h_low(k, gain, count):
                dve.wait_ge(rhs_hi, count)
                dve.scalar_tensor_tensor(out=row(h_lo, k), in0=row(x_sb, k),
                                         scalar=chan[:, ds(gain + k, 1)],
                                         in1=row(h_hi, k).bitcast(f32),
                                         op0=ALU.mult, op1=ALU.subtract).then_inc(rhs_ready, 1)

            lo(0, [0])
            dve.wait_ge(chan_ready, 16)
            for part, (k0, k1) in enumerate(X_PARTS):
                if part > 2:
                    lo(0, [k0 // 4])
                dve.wait_ge(in_ready[part], 16)
                if k1 - k0 < 4:
                    for k in range(k0, k1):
                        h_low(k, C_MIXPRE, k + 1)
                else:
                    with dve.Fori(0, 4) as i:
                        h_low(k0 + i, C_MIXPRE, k0 + i + 1)
            dve.wait_ge(tab_ready, 16 * 10)
            for nb, wcol, state, dst in ((KA, C_CONVW, cst_sb, cs_s), (KF, C_FCONVW, fst_sb, fs_s)):
                st.wait()
                for j, o_ in ((0, dst), (1, cst_tmp)):
                    st.done(dve.tensor_tensor(
                        o_[:, 0:nb, :], state[:, :, :, j],
                        chan[:, wcol + nb * j:wcol + nb * (j + 1)].unsqueeze(2)
                        .to_broadcast([P, nb, TS]), ALU.mult))
                st.wait()
                st.done(dve.tensor_tensor(dst[:, 0:nb, :], dst[:, 0:nb, :], cst_tmp[:, 0:nb, :],
                                          ALU.add))
            lo(1)
            invert(0)
            complete(0)
            dve.wait_ge(rstd_ready, 1)
            scaled(rope_in[0][:, :], 0).then_inc(acc_free, 1)
            st.done(dve.tensor_tensor(rstd2[:, :], rstd[:, :], rstd[:, :], ALU.mult))

            def sine(r):
                dve.wait_ge(rope_rot, r + 1)
                if not (isinstance(r, int) and r == 0):
                    dve.wait_ge(rope_done, r)
                dve.tensor_tensor(two(rope_s[:, :]), both(3), two(sin[:, :]), ALU.mult)\
                   .then_inc(rope_sin, 1)
            lo(2)
            complete(1)
            scaled(vT_sb[:, :], 1).then_inc(acc_free, 1)
            sine(0)
            dve.wait_ge(v_turned, 1)
            st.done(dve.tensor_copy(v_tok[:, 1:NB + 1, :], bank[0].rearrange("p (b s) -> p b s", b=NB)))
            dve.tensor_copy(v_new[:, :], bank[1][0:TS, 0:P]).then_inc(v_stored, 1)

            def q_pair(i, first):
                for u in range(2):
                    t = 2 * i + u
                    lo(Q_Q + 1 + t)
                    complete(Q_Q + t)
                    dve.wait_ge(rope_done, t if not first else max(t, 1))
                    scaled(rope_in[(u + 1) % 2][:, :], u).then_inc(acc_free, 1)
                    if not (first and u == 0):
                        sine(t)
            q_pair(0, True)
            with dve.Fori(1, KA // 2) as i:
                q_pair(i, False)
            sine(KA)

            dve.wait_ge(rope_done, 1)
            dve.tensor_copy(k_cache[:, :, 0], kT_sb[:, BLK + TP:BLK + T]).then_inc(k_placed, 1)
            lo(Q_CONV + 1, range(3))
            dve.wait_ge(ss_ready, 1)
            dve.wait_ge(pool_set, 5)
            for r in (0, 32):
                st.done(dve.tensor_scalar(ss_sb[r:r + GRP, :, :],
                                          bank[0][r:r + GRP, :].rearrange("p (n s) -> p n s", n=TS // 2),
                                          SCALE, None, ALU.mult))
            st.wait()
            dve.wait_ge(ss_scaled, 2)
            sm = small[0:SR, :, 0:TS // 2]
            st.done(dve.tensor_reduce(sm[:, 0, :], ss_sb[:, :, :], AX.X, ALU.max))
            st.wait()
            st.done(dve.tensor_scalar(sm[:, 0, :], sm[:, 0, :], sinks[0:SR, :], None, ALU.max))
            st.wait()
            dve.tensor_scalar(sm[:, 1, :], sm[:, 0, :], -1.0, sinks[0:SR, :], ALU.mult, ALU.add)\
               .then_inc(ss_shift, 1)

            def per_row(col):
                return sm[:, col, :].unsqueeze(2).to_broadcast([SR, TS // 2, BLK])
            dve.tensor_tensor(ss_sb[:, :, :], ss_sb[:, :, :], per_row(0), ALU.subtract)\
               .then_inc(ss_shift, 1)
            def masked_scores(i, u):
                if u == 0:
                    dve.wait_ge(mask_ready, 16 * i + 16)
                for n, j in enumerate((1, 2, 3, 0)):
                    g, th = j // 2, j % 2
                    wait_alone(dve, s_ready, 8 * i + (4 * u + n + 1))
                    for v in range(2):
                        h = 4 * g + 2 * th + v
                        ins = dve.tensor_tensor_reduce(
                            s_sb[:, h, :], bank[j][:, v * 256:(v + 1) * 256], mask_blk[:, :],
                            SCALE, -3.0e38, ALU.add, ALU.max, small[:, 0, h:h + 1])
                st.done(ins)
                st.wait()
                sk = sinkp[:, 8 * u:8 * u + 8]
                st.done(dve.tensor_tensor(small[:, 0, 0:8], small[:, 0, 0:8], sk, ALU.max))
                st.wait()
                st.done(dve.tensor_scalar(small[:, 1, 0:8], small[:, 0, 0:8], -1.0, None, ALU.mult))
                dve.tensor_tensor(small[:, 2, 0:8], sk, small[:, 0, 0:8], ALU.subtract)\
                   .then_inc(m_ready, 1)

            def c_out(i, u):
                q = Q_CONV + 6 * i + 3 * u
                complete(q)
                scaled(c_sb[:, :], (3 * u) % 2, rstd2).then_inc(acc_free, 1)

            def probabilities(i, u):
                j2 = 2 * i + u
                dve.wait_ge(e_ready, j2 + 1)
                st.done(dve.tensor_tensor(small[:, 3, 0:8], small[:, 3, 0:8], small[:, 4, 0:8],
                                          ALU.add))
                st.wait()
                st.done(dve.reciprocal(small[:, 5, 0:8], small[:, 3, 0:8]))
                st.wait()
                dve.tensor_tensor(s_sb[:, :, :], s_sb[:, :, :],
                                  small[:, 5, 0:8].unsqueeze(2).to_broadcast([P, 8, 2 * BLK]),
                                  ALU.mult).then_inc(prob_ready, 1)

            def z_conv(i, u):
                q = Q_CONV + 6 * i + 3 * u
                m = M_CONV + 6 * i + 3 * u
                j2 = 2 * i + u
                complete(q + 1)
                dve.wait_ge(acc_free, m + 1)
                scaled(zb[:, 2:T + 2], (3 * u + 1) % 2, c_sb).then_inc(acc_free, 1)
                dve.wait_ge(acc_free, m + 2)
                st.done(dve.tensor_scalar(cv[:, 0:TP], zb[:, 0:TP],
                                          chan[:, ds(C_CONVW + j2, 1)], None, ALU.mult))
                st.wait()
                st.done(dve.scalar_tensor_tensor(out=cv[:, 0:TP], in0=zb[:, 1:TP + 1],
                                                 scalar=chan[:, ds(C_CONVW + KA + j2, 1)],
                                                 in1=cv[:, 0:TP], op0=ALU.mult, op1=ALU.add))
                st.wait()
                st.done(dve.scalar_tensor_tensor(out=cv[:, 0:TP], in0=zb[:, 2:TP + 2],
                                                 scalar=chan[:, ds(C_CONVW + 2 * KA + j2, 1)],
                                                 in1=cv[:, 0:TP], op0=ALU.mult, op1=ALU.add))
                st.done(dve.scalar_tensor_tensor(out=cv[:, TP:T], in0=zb[:, TP + 2:T + 2],
                                                 scalar=chan[:, ds(C_CONVW + 2 * KA + j2, 1)],
                                                 in1=row(cs_s, j2), op0=ALU.mult, op1=ALU.add))
                dve.tensor_copy(row(ctail, j2), zb[:, TP:T + 2])
                st.wait()
                st.done(dve.tensor_tensor(cv[:, :], cv[:, :], rstd[:, :], ALU.mult))

            def turned(i, u):
                for j in range(2):
                    dve.wait_ge(pT_ready, 8 * i + (4 * u + j + 3))
                    dve.tensor_copy(pT_sb[:, 2 + j, :], bank[2 + j]).then_inc(pT_dve, 1)

            def b_conv(i, u):
                q = Q_CONV + 6 * i + 3 * u
                complete(q + 2)
                st.wait()
                scaled(bt[:, :], (3 * u + 2) % 2, cv).then_inc(acc_free, 1)

            def conv_low(i, u):
                j2 = 2 * i + u
                dve.wait_ge(b_hi_ready, j2 + 1)
                dve.tensor_tensor(row(b_lo, j2), bt[:, :], row(b_hi, j2).bitcast(f32),
                                  ALU.subtract).then_inc(b_ready, 1)

            def attention_low(i, u):
                j2 = 2 * i + u
                dve.wait_ge(a_hi_ready, j2 + 1)
                dve.tensor_tensor(a_lo[:, 4 * u:4 * u + 4, ds(i * BLK, BLK)],
                                  bank[0].rearrange("p (t s) -> p t s", t=4),
                                  a_hi[:, 4 * u:4 * u + 4, ds(i * BLK, BLK)].bitcast(f32),
                                  ALU.subtract).then_inc(a_ready, 1)

            lo(Q_CONV + 1, [3])
            c_out(0, 0)
            dve.wait_ge(ss_exp, 2)
            st.done(dve.tensor_reduce(sm[:, 3, :], ss_sb[:, :, :], AX.X, ALU.add))
            st.wait()
            st.done(dve.tensor_tensor(sm[:, 3, :], sm[:, 3, :], sm[:, 2, :], ALU.add))
            st.wait()
            st.done(dve.reciprocal(sm[:, 4, :], sm[:, 3, :]))
            st.wait()
            dve.tensor_tensor(ss_sb[:, :, :], ss_sb[:, :, :], per_row(4), ALU.mult)\
               .then_inc(ss_prob, 1)
            lo(Q_CONV + 2, range(2))
            dve.wait_ge(ss_turned, 1)
            dve.tensor_copy(pTs_sb[:, :, :],
                            bank[1][:, 0:TS // 2 * SR].rearrange("p (a b) -> p a b", a=TS // 2))\
               .then_inc(ss_copied, 1)
            lo(Q_CONV + 2, [2])
            dve.wait_ge(ss_hi, 1)
            dve.tensor_tensor(a_lo[:, :, TP:T],
                              bank[0][:, 0:TS * GRP].rearrange("p (n t) -> p t n", n=TS),
                              a_hi[:, :, TP:T].bitcast(f32), ALU.subtract).then_inc(a_ready, 1)

            PER = 2 * 10
            lo(Q_CONV + 2, [3])
            z_conv(0, 0)
            masked_scores(0, 0)
            probabilities(0, 0)
            lo(Q_CONV + 3)
            b_conv(0, 0)
            turned(0, 0)
            conv_low(0, 0)
            attention_low(0, 0)

            def half_block(i, u):
                q = Q_CONV + 6 * i + 3 * u
                masked_scores(i, u)
                lo(q + 1)
                c_out(i, u)
                probabilities(i, u)
                lo(q + 2)
                z_conv(i, u)
                turned(i, u)
                lo(q + 3)
                b_conv(i, u)
                conv_low(i, u)
                attention_low(i, u)
            half_block(0, 1)
            base = st.base + st.k - PER
            with dve.Fori(1, NB) as i:
                st.at(base + PER * i)
                half_block(i, 0)
                half_block(i, 1)
                assert st.k == PER, st.k
            base += NB * PER

            def m_low(k):
                dve.wait_ge(rhs_hi, KD + k + 1)
                dve.tensor_tensor(h_lo[:, k, :], merged[:, k, :], h_hi[:, k, :].bitcast(f32),
                                  ALU.subtract).then_inc(rhs_ready, 1)

            def gates(i, last=False):
                q = Q_MERGE + 3 * i
                for j, gate in enumerate((ga_sb, gb_sb)):
                    lo(q + (1 + j))
                    complete(q + j)
                    scaled(gate[:, :], j).then_inc(acc_free, 1)
                for j, (gate, part) in enumerate(((ga_sb, ma_sb), (gb_sb, mb_sb))):
                    for g in range(2 * j, 2 * j + 2):
                        lo(q + 3, [g])
                        if last:
                            for k in range(4 * g, 4 * g + 4 if g < 3 else 4 * g):
                                m_low(k)
                    dve.wait_ge(gate_out, 2 * i + (j + 1))
                    dve.wait_ge(w_used, 4 * q + (10 + 2 * j))
                    scaled(part[:, :], j, gate).then_inc(acc_free, 1)
                dve.wait_ge(acc_free, M_MERGE + 4 * i + 4)
                dve.tensor_tensor(row(merged, i), ma_sb[:, :], mb_sb[:, :], ALU.add)\
                   .then_inc(merged_ready, 1)
            with dve.Fori(0, KD - 1) as i:
                gates(i)
            gates(KD - 1, last=True)
            for k in range(3 * KD // 4, KD):
                m_low(k)

            with dve.Fori(0, KD // 2) as i:
                for u in range(2):
                    m = 2 * i + u
                    lo(Q_O + 1 + m)
                    complete(Q_O + m)
                    dve.tensor_copy(two(row(y_sb, m)), both(u)).then_inc(acc_free, 1)
            st.at(base)
            invert(1)
            base += 1
            dve.wait_ge(rstd_ready, 2)
            dve.wait_ge(x_back, 16)

            def new_x(n, gain, low, between=None):
                def product(i):
                    for u in range(2):
                        k = 2 * i + u
                        if not (isinstance(i, int) and i == 0):
                            dve.wait_ge(x_new, k + (n - 1))
                        dve.scalar_tensor_tensor(out=tt[u][:, :], in0=row(y_sb, k),
                                                 scalar=chan[:, ds(gain + k, 1)],
                                                 in1=rstd[:, :], op0=ALU.mult, op1=ALU.mult)\
                           .then_inc(xy_ready, 1)
                product(0)
                if between is None:
                    with dve.Fori(1, KD // 2) as i:
                        product(i)
                        low(2 * i - 2)
                        low(2 * i - 1)
                else:
                    for i in range(1, KD // 2):
                        product(i)
                        low(2 * i - 2)
                        low(2 * i - 1)
                        if i in between:
                            between[i]()
                low(KD - 2)
                low(KD - 1)
            new_x(0, C_MIXPOST, lambda k: h_low(k, C_FFNPRE, k + (2 * KD + 1)))

            PERT = 5

            def up(c, t, start, first=False):
                q = Q_FFN + Q_CHUNK * c + 2 * t
                tile = CH * c + t
                lo(q + 1, range(3))
                if first:
                    st.at(base)
                    invert(2)
                    dve.wait_ge(rstd_ready, 3)
                    dve.wait_ge(pool_set, 6)
                st.at(start + PERT * tile)
                complete(q)
                scaled(fzb[:, 2:T + 2], 0).then_inc(acc_free, 1)
                lo(q + 1, [3])
                dve.wait_ge(acc_free, M_FFN + M_CHUNK * c + 2 * t + 1)
                st.done(dve.tensor_scalar(fcv[:, 0:TP], fzb[:, 0:TP],
                                          chan[:, ds(C_FCONVW + tile, 1)], None, ALU.mult))
                st.wait()
                st.done(dve.scalar_tensor_tensor(out=fcv[:, 0:TP], in0=fzb[:, 1:TP + 1],
                                                 scalar=chan[:, ds(C_FCONVW + KF + tile, 1)],
                                                 in1=fcv[:, 0:TP], op0=ALU.mult, op1=ALU.add))
                st.wait()
                st.done(dve.scalar_tensor_tensor(out=fcv[:, TP:T], in0=fzb[:, TP + 2:T + 2],
                                                 scalar=chan[:, ds(C_FCONVW + 2 * KF + tile, 1)],
                                                 in1=row(fs_s, tile), op0=ALU.mult, op1=ALU.add))
                dve.scalar_tensor_tensor(out=fcv[:, 0:TP], in0=fzb[:, 2:TP + 2],
                                         scalar=chan[:, ds(C_FCONVW + 2 * KF + tile, 1)],
                                         in1=fcv[:, 0:TP], op0=ALU.mult, op1=ALU.add)\
                   .then_inc(fconv_ready, 1)
                st.done(dve.tensor_copy(row(ftail, tile), fzb[:, TP:T + 2]))
                dve.wait_ge(gelu_ready, tile + 1)
                st.done(dve.tensor_tensor(ge2[:, :], ge[:, :], rstd[:, :], ALU.mult))
                lo(q + 2, range(3))
                complete(q + 1)
                st.wait()
                scaled(ft[:, :], 1, ge2).then_inc(acc_free, 1)
                dve.wait_ge(f_hi_ready, tile + 1)
                dve.tensor_tensor(row(f_lo, t), ft[:, :], row(f_hi, t).bitcast(f32),
                                  ALU.subtract).then_inc(f_ready, 1)
                lo(q + 2, [3])
                assert st.k == PERT, st.k

            def down(c):
                with dve.Fori(0, KD // 4) as j:
                    q = Q_FFN + Q_CHUNK * c + j + 2 * CH
                    for g in range(4):
                        dve.wait_ge(w_used, 4 * q + (g + 1))
                        yr = two(row(y_sb, 4 * j + g))
                        dve.tensor_tensor(yr, both(g % 2), yr, ALU.add).then_inc(acc_free, 1)
                        lo(q + 1, [g])
            start = base + 1
            up(0, 0, start, first=True)
            with dve.Fori(1, CH) as t:
                up(0, t, start)
            for k in range(KP):
                dve.wait_ge(p_split_hi, k + 1)
                dve.tensor_tensor(p_lo[:, k, :], p_raw[:, k, :], p_hi[:, k, :].bitcast(f32),
                                  ALU.subtract).then_inc(p_split, 1)
            dve.wait_ge(y_clear, 1)
            down(0)
            with dve.Fori(1, NCH) as c:
                with dve.Fori(0, CH) as t:
                    up(c, t, start)
                down(c)
            base = start + PERT * KF

            lo(Q_PLE + 1, [0])
            st.at(base)
            invert(3)
            lo(Q_PLE + 1, [1])
            dve.wait_ge(rstd_ready, 4)

            def x_low(k):
                dve.wait_ge(rhs_hi, k + (3 * KD + 1))
                dve.tensor_tensor(row(h_lo, k), row(x_sb, k), row(h_hi, k).bitcast(f32),
                                  ALU.subtract).then_inc(rhs_ready, 1)
            new_x(KD, C_FFNPOST, x_low, {1: lambda: lo(Q_PLE + 1, [2]),
                                         2: lambda: lo(Q_PLE + 1, [3]),
                                         4: lambda: lo(Q_GATE, [0]), 5: lambda: lo(Q_GATE, [1]),
                                         6: lambda: lo(Q_GATE, [2]), 7: lambda: lo(Q_GATE, [3])})

            def gate(i, u, first=False, last=False):
                m = 2 * i + u
                if not last:
                    lo(Q_GATE + 1 + m)
                dve.wait_ge(acc_free, M_GATE + m + 1)
                if not first:
                    dve.wait_ge(x_out, m)
                dve.tensor_tensor(tt[1][:, :], tt[0][:, :], row(ple_sb, m), ALU.mult)\
                   .then_inc(sig_used, 1)
                dve.wait_ge(sig_used, m + 1)
                dve.tensor_tensor(row(x_sb, m), row(x_sb, m), tt[1][:, :], ALU.add)\
                   .then_inc(x_out, 1)
            gate(0, 0, first=True)
            gate(0, 1)
            with dve.Fori(1, KD // 2 - 1) as i:
                gate(i, 0)
                gate(i, 1)
            gate(KD // 2 - 1, 0)
            gate(KD // 2 - 1, 1, last=True)

        @block.gpsimd
        def _(pool):
            def add_squares(n, bufs, acc):
                with pool.Fori(0, KD // 2) as i:
                    for u in range(2):
                        pool.wait_ge(sq_ready, 16 * n + 2 * i + (u + 1))
                        pool.wait_ge(sq_added, 16 * n + 2 * i + (u + 1))
                        pool.tensor_tensor(acc[:, :], acc[:, :], bufs[u][:, :], ALU.add)\
                            .then_inc(sq_added, 1)

            pool.memset(sqacc1[:, :], 0.0).then_inc(sq_added, 1)
            pool.memset(kT_sb[:, 0:BLK], 0.0).then_inc(pool_set, 1)
            pool.memset(v_tok[:, 0, :], 0.0).then_inc(pool_set, 1)
            pool.memset(ones[:, :], 1.0).then_inc(pool_set, 1)
            pool.wait_ge(pool_set, 3)
            add_squares(0, sq_a, sqacc1)
            pool.memset(ss_sb[:, :, :], 0.0).then_inc(pool_set, 1)
            pool.memset(zb[:, 0:2], 0.0).then_inc(pool_set, 1)

            def cosine(r, src, dst):
                pool.wait_ge(acc_free, rope_tile(r))
                if not (isinstance(r, int) and r == 0):
                    pool.wait_ge(rope_done, r)
                pool.tensor_tensor(rope_c[:, :], src[:, :], cos[:, :], ALU.mult).then_inc(rope_cos, 1)
                pool.wait_ge(rope_cos, r + 1)
                pool.wait_ge(rope_sin, r + 1)
                pool.tensor_tensor(dst, rope_c[:, :], rope_s[:, :], ALU.add).then_inc(rope_done, 1)
            pool.wait_ge(tab_ready, 16 * 10)
            cosine(0, rope_in[0], kT_sb[:, BLK:BLK + T])
            pool.wait_ge(rope_done, 1)
            pool.dma_start(kT_out, kT_sb[:, TP:BLK + T]).then_inc(tail_out, 16)
            pool.wait_ge(acc_free, 2)
            pool.dma_start(vT_out, vT_sb[:, TP - BLK:T]).then_inc(tail_out, 16)
            pool.wait_ge(v_stored, 1)
            pool.dma_start(v_cache[0:1, :, :], v_new[:, :]).then_inc(v_placed, 16)
            with pool.Fori(0, KA // 2) as i:
                for u in range(2):
                    cosine(2 * i + (u + 1), rope_in[(u + 1) % 2], row(q_sb, 2 * i + u))

            def stage_qk(i):
                pool.dma_start(mask_blk[:, :], mask_in[ds(i, 1), :, :].rearrange("a p n -> (a p) n"))\
                    .then_inc(mask_ready, 16)
                pool.tensor_copy(q_blk[:, :, :], q_sb[:, :, ds(i * BLK, BLK)]).then_inc(staged_qk, 1)
                pool.tensor_copy(k_blk[:, :], kT_sb[:, ds(i * BLK, 2 * BLK)]).then_inc(staged_qk, 1)

            def stage_v(i):
                pool.tensor_copy(v_blk[:, :, :], v_tok[:, ds(i, 2), :]).then_inc(staged_v, 1)
            pool.wait_ge(rope_done, KA + 1)
            stage_qk(0)
            stage_v(0)
            pool.wait_ge(v_placed, 16)
            with pool.Fori(1, NB) as i:
                pool.wait_ge(s_ready, 8 * i)
                pool.wait_ge(m_ready, 2 * i)
                stage_qk(i)
                pool.wait_ge(a_ready, 2 * i + 1)
                stage_v(i)

            pool.wait_ge(w_used, 4 * Q_O)
            pool.dma_start(x_sb[:, :, :], x_in).then_inc(x_back, 16)
            pool.wait_ge(merged_ready, KD)
            pool.memset(sqacc2[:, :], 0.0).then_inc(acc_zero, 1)
            pool.wait_ge(rhs_ready, 2 * KD)
            pool.dma_start(p_raw[:, :, :], p_in).then_inc(p_ready, 16)
            pool.memset(fzb[:, 0:2], 0.0).then_inc(pool_set, 1)
            pool.wait_ge(acc_zero, 1)
            add_squares(1, sq_b, sqacc2)

            def add_to_x(n):
                with pool.Fori(0, KD // 2) as i:
                    for u in range(2):
                        k = 2 * i + u
                        pool.wait_ge(xy_ready, k + (n + 1))
                        pool.tensor_tensor(row(x_sb, k), row(x_sb, k), tt[u][:, :], ALU.add)\
                            .then_inc(x_new, 1)
            pool.wait_ge(x_back, 16)
            add_to_x(0)
            pool.memset(y_sb[:, :, :], 0.0).then_inc(y_clear, 1)
            pool.wait_ge(p_split, KP)
            pool.memset(sqacc3[:, :], 0.0).then_inc(acc_zero, 1)
            pool.wait_ge(acc_zero, 2)
            add_squares(2, sq_c, sqacc3)
            add_to_x(KD)
            pool.dma_start(ctail_out, ctail[:, :, :]).then_inc(tail_out, 16)
            pool.dma_start(ftail_out, ftail[:, :, :]).then_inc(tail_out, 16)
            with pool.Fori(0, KD) as m:
                pool.wait_ge(x_out, m + 1)
                pool.dma_start(y_out[ds(m, 1), :, :].rearrange("a p n -> (a p) n"), row(x_sb, m))\
                    .then_inc(out_done, 16)
            pool.wait_ge(out_done, 16 * KD)
            pool.wait_ge(tail_out, 16 * 4)


def _blocks(w, cols):
    k = w.shape[0] // P
    w = w[:, cols] if cols is not None else w
    return w.reshape(k, P, w.shape[1] // P, P).transpose(2, 0, 1, 3)


def _slots(blocks):
    n = blocks.reshape(-1, 4, P, P)
    return n.transpose(0, 2, 1, 3).reshape(-1, P, 4 * P)


def kernel(**inputs):
    import concourse.bacc as bacc
    from concourse.bass_utils import run_bass_kernel_spmd

    v = {n: np.asarray(a) for n, a in inputs.items()}
    f = np.float32
    pairs = np.concatenate([np.r_[HD * t:HD * t + HD, HD * (t + GRP):HD * (t + GRP) + HD]
                            for t in range(GRP)])
    w_in, up, down = v["w_in"][0], v["w_ffn_up"][0], v["w_ffn_down"][0]
    qw, kvw = w_in[:, 0:NH * HD], w_in[:, NH * HD:NH * HD + 2 * P]
    c0 = NH * HD + 2 * P
    cw = KA * P
    kv = _blocks(kvw, None)
    conv = np.stack([_blocks(w_in[:, c0 + o:c0 + o + cw], None) for o in (cw, 2 * cw, 0)], 1)
    ga = _blocks(w_in[:, c0 + 3 * cw:c0 + 3 * cw + D], None)
    gb = _blocks(w_in[:, c0 + 3 * cw + D:c0 + 3 * cw + 2 * D], None)
    br = np.concatenate([_blocks(v["w_attn_branch"][0][pairs], None),
                         _blocks(v["w_conv_branch"][0], None)], 1)
    merge = np.stack([ga, gb, br], 1)
    fa, fg = _blocks(up[:, :FF], None), _blocks(up[:, FF:], None)
    fd = _blocks(down, None)
    stream = [_slots(kv), _slots(_blocks(qw, pairs)), _slots(conv), _slots(merge),
              _slots(_blocks(v["w_o"][0], None))]
    for c in range(NCH):
        s = slice(CH * c, CH * c + CH)
        stream += [_slots(np.stack([fa[s], fg[s]], 1)), _slots(fd[:, s])]
    stream += [_slots(_blocks(v["w_ple"][0], None)), _slots(_blocks(v["w_ple_gate"][0], None))]
    wstream = np.concatenate(stream).reshape(NQ, 4, P, 4 * P)

    def fmajor(a):
        return a.T.reshape(a.shape[1] // P, P, a.shape[0]).transpose(1, 0, 2)

    def cols(a):
        return a.reshape(a.shape[0], -1, P).transpose(2, 0, 1).reshape(P, -1)
    x = fmajor(np.concatenate([v["x_prompt"][0], v["x_sample"][:, 0]]))
    p = fmajor(np.concatenate([v["p_prompt"][0, 0], v["p_sample"][0, :, 0]]))
    chan = np.concatenate([cols(v["norm_mix_pre"]), cols(v["norm_mix_post"]),
                           cols(v["norm_ffn_pre"]), cols(v["norm_ffn_post"]),
                           cols(v["conv_w"][0]), cols(v["b_gate"][0]),
                           cols(v["ffn_conv_w"][0]), cols(v["ffn_conv_b"])], 1)
    sk = v["attn_sinks"][0].reshape(NKV, 2, 4)
    sinkp = np.broadcast_to(sk.transpose(1, 0, 2).reshape(1, NH), (P, NH))
    sinks = np.zeros((P, 1), f)
    for quadrant in range(4):
        g0 = GRP * (quadrant // 2)
        sinks[32 * quadrant:32 * quadrant + GRP, 0] = v["attn_sinks"][0][g0:g0 + GRP]

    def state(a, k):
        return a.reshape(TS, 2, k, P).transpose(3, 2, 0, 1)
    ks = v["state_attn_k"][0].reshape(TS, BLK, P)
    vs = v["state_attn_v"][0].reshape(TS, BLK, P)
    eye = np.eye(P, dtype=f)
    rot = np.zeros((P, P), f)
    for h in range(2):
        for d in range(HD // 2):
            rot[HD * h + HD // 2 + d, HD * h + d] = -1.0
            rot[HD * h + d, HD * h + HD // 2 + d] = 1.0
    inv = (f(10000.0) ** (-np.arange(HD // 2, dtype=f) / f(HD // 2))).astype(f)
    pos = np.concatenate([np.arange(TP), np.full(TS, 2048)]).astype(f)
    ang = (pos[None, :] * inv[:, None]).astype(f)
    rots = np.stack([np.tile(np.cos(ang), (4, 1)), np.tile(np.sin(ang), (4, 1))]).astype(f)
    qi, ci = np.arange(BLK)[:, None], np.arange(2 * BLK)[None, :]
    rel = BLK + qi - ci
    band = (rel >= 0) & (rel < BLK)
    mask = np.stack([np.where(band & ((b > 0) | (ci >= BLK)), 0.0, -1e30) for b in range(NB)])

    feeds = dict(
        wstream=wstream, x=x, p=p, chan=chan, sinkp=sinkp, sinks=sinks,
        cstate=state(v["state_conv"][0], KA), fstate=state(v["state_ffn_conv"][0], KF),
        kcache=ks[:, 1:].transpose(2, 0, 1), vcache=vs[:, 1:].transpose(1, 0, 2),
        kstate=ks[:, 1:], vstate=vs[:, 1:],
        cst1=v["state_conv"][0][:, 1], fst1=v["state_ffn_conv"][0][:, 1],
        mats=np.stack([eye, rot]), rots=rots, mask=mask.astype(f))
    outs = dict(y=(KD, P, T), kT=(P, BLK + TS), vT=(P, BLK + TS), ctail=(P, KA, TS + 2),
                ftail=(P, KF, TS + 2), kold=(TS, BLK - 1, P), vold=(TS, BLK - 1, P),
                cold=(TS, KA * P), fold=(TS, FF))

    nc = bacc.Bacc("TRN2", target_bir_lowering=False, num_devices=1)
    arrays, args = {}, []
    for name, a in feeds.items():
        arrays[f"in_{name}"] = np.ascontiguousarray(a)
        args.append(nc.dram_tensor(f"in_{name}", list(a.shape), mybir.dt.from_np(a.dtype),
                                   kind="ExternalInput").ap())
    for name, shape in outs.items():
        args.append(nc.dram_tensor(f"out_{name}", list(shape), mybir.dt.float32,
                                   kind="ExternalOutput").ap())
    build(nc, *args)
    r = run_bass_kernel_spmd(nc, [arrays], core_ids=[0]).results[0]
    g = {n: np.asarray(r[f"out_{n}"]) for n in outs}

    def tmajor(a):
        return a.transpose(2, 1, 0).reshape(a.shape[2], -1)
    y = g["y"].reshape(D, T).T
    kt, vt = g["kT"].T, g["vT"].T
    ct, ft = tmajor(g["ctail"]), tmajor(g["ftail"])

    def new_state(old, new):
        return np.concatenate([old, new], 1)
    kn, vn = (new_state(o, t[BLK:, None]).reshape(1, TS, BLK, NKV, HD)
              for o, t in ((g["kold"], kt), (g["vold"], vt)))
    cn, fn = (new_state(o[:, None], t[2:, None])[None] for o, t in ((g["cold"], ct), (g["fold"], ft)))
    c = np.ascontiguousarray
    return (c(y[:TP])[None], c(y[TP:])[:, None],
            c(kt[:BLK]).reshape(1, 1, BLK, NKV, HD), c(vt[:BLK]).reshape(1, 1, BLK, NKV, HD),
            c(ct[:2])[None, None], c(ft[:2])[None, None], kn, vn, cn, fn)
```
